# Optimizing a Trainium2 kernel written in Bass

```python
import math
import jax
import jax.numpy as jnp
from jax import lax
import numpy as np

D_MODEL = 2048
BATCH = 1
SEQ = 256
DEPTH = 2

GRID_W = 64
CTX_LEN = 256
D_MIX = D_MODEL
A_HEADS = 8
A_HEAD_DIM = 64
A_VAL_DIM = 2 * A_HEAD_DIM
QK_A = A_HEADS * 2 * A_HEAD_DIM
V_A = A_HEADS * A_VAL_DIM
B_HEADS = 8
B_DK = 128
B_DV = 128
QK_B = B_HEADS * B_DK
V_B = B_HEADS * B_DV
CONV_K = 5
CONV_CH = 2 * QK_B + V_B
CHUNK = 64
Q_BLOCK = 128
ROPE_THETA = 10000.0
NORM_EPS = 1e-6
SUBLN_EPS = 1e-5
N_IN = 2 * QK_A + 2 * V_A + CONV_CH + V_B + 4 * B_HEADS

kernel_name = 'hybrid_diffattn_gdn_prefix_trunk'

def rmsnorm(x, w, eps=NORM_EPS):
    xf = x.astype(jnp.float32)
    y = xf * lax.rsqrt(jnp.mean(xf * xf, axis=-1, keepdims=True) + eps)
    return (y * w.astype(jnp.float32)).astype(x.dtype)

def l2norm(x, eps=1e-6):
    xf = x.astype(jnp.float32)
    return xf * lax.rsqrt(jnp.sum(xf * xf, axis=-1, keepdims=True) + eps)

def split_in(p):
    sizes = (QK_A, QK_A, V_A, V_A, CONV_CH, V_B, 4 * B_HEADS)
    points = np.cumsum(sizes)[:-1].tolist()
    return jnp.split(p, points, axis=-1)

def axial_rope(rows, cols):
    n_freq = A_HEAD_DIM // 4
    inv = ROPE_THETA ** (-jnp.arange(n_freq, dtype=jnp.float32) / n_freq)
    ang = jnp.concatenate([rows[:, None] * inv, cols[:, None] * inv], axis=-1)
    return jnp.cos(ang), jnp.sin(ang)

def apply_rope(t, cos, sin):
    t1, t2 = jnp.split(t, 2, axis=-1)
    c = cos[None, :, None, :]
    s = sin[None, :, None, :]
    return jnp.concatenate([t1 * c - t2 * s, t1 * s + t2 * c], axis=-1).astype(t.dtype)

def qk_heads(t, cos=None, sin=None):
    bsz, n, _ = t.shape
    t = t.reshape(bsz, n, A_HEADS * 2, A_HEAD_DIM)
    if cos is not None:
        t = apply_rope(t, cos, sin)
    return t.reshape(bsz, n, A_HEADS, 2, A_HEAD_DIM).transpose(0, 2, 3, 1, 4)

def v_heads(t):
    bsz, n, _ = t.shape
    return t.reshape(bsz, n, A_HEADS, A_VAL_DIM).transpose(0, 2, 1, 3)

def diff_attend(q, k, v, lam):
    s = jnp.einsum('bhmqd,bhmkd->bhmqk', q, k).astype(jnp.float32) * (A_HEAD_DIM ** -0.5)
    p = jax.nn.softmax(s, axis=-1)
    a = p[:, :, 0] - lam * p[:, :, 1]
    return jnp.einsum('bhqk,bhkd->bhqd', a.astype(v.dtype), v)

def diff_attend_blocked(q, k, v, lam):
    bsz, h, _, n_q, d = q.shape
    nb = n_q // Q_BLOCK
    qb = q.reshape(bsz, h, 2, nb, Q_BLOCK, d).transpose(3, 0, 1, 2, 4, 5)
    ob = lax.map(lambda qq: diff_attend(qq, k, v, lam), qb)
    return ob.transpose(1, 2, 0, 3, 4).reshape(bsz, h, n_q, A_VAL_DIM)

def diff_post(o, subln_w, lam_init, z):
    bsz, _, n, _ = o.shape
    o = rmsnorm(o, subln_w, SUBLN_EPS) * (1.0 - lam_init)
    o = o.transpose(0, 2, 1, 3).reshape(bsz, n, V_A)
    return (o * jax.nn.silu(z)).astype(z.dtype)

def centred_dwconv(x, w):
    k = w.shape[0]
    return lax.conv_general_dilated(
        x, w[:, None, :].astype(x.dtype), window_strides=(1,),
        padding=[((k - 1) // 2, k // 2)],
        dimension_numbers=('NWC', 'WIO', 'NWC'),
        feature_group_count=x.shape[-1])

def delta_prep(qkv, ab, conv_w, a_log, dt_bias):
    bsz, n, _ = qkv.shape
    qkv = jax.nn.silu(centred_dwconv(qkv, conv_w))
    q, k, v = jnp.split(qkv, [QK_B, 2 * QK_B], axis=-1)
    q = l2norm(q.reshape(bsz, n, B_HEADS, B_DK)).transpose(0, 2, 1, 3)
    k = l2norm(k.reshape(bsz, n, B_HEADS, B_DK)).transpose(0, 2, 1, 3)
    v = v.reshape(bsz, n, B_HEADS, B_DV).transpose(0, 2, 1, 3).astype(jnp.float32)
    ab = ab.astype(jnp.float32).reshape(bsz, n, 2, 2, B_HEADS).transpose(2, 3, 0, 4, 1)
    a_log = a_log.astype(jnp.float32)
    dt_bias = dt_bias.astype(jnp.float32)
    g = -jnp.exp(a_log)[:, None, :, None] * jax.nn.softplus(ab[0] + dt_bias[:, None, :, None])
    beta = jax.nn.sigmoid(ab[1])
    return q, k, v, g, beta

def gated_delta_chunked(q, k, v, g, beta, s0):
    bsz, h, n, dk = q.shape
    dv = v.shape[-1]
    nc = n // CHUNK
    q = q * (dk ** -0.5)
    rs = lambda t: t.reshape(bsz, h, nc, CHUNK, *t.shape[3:])
    q, k, v, g, beta = rs(q), rs(k), rs(v), rs(g), rs(beta)
    g = jnp.cumsum(g, axis=-1)
    tri = jnp.tril(jnp.ones((CHUNK, CHUNK), dtype=bool))
    tri_strict = jnp.tril(jnp.ones((CHUNK, CHUNK), dtype=bool), -1)
    diff = g[..., :, None] - g[..., None, :]
    decay = jnp.where(tri, jnp.exp(jnp.where(tri, diff, 0.0)), 0.0)
    k_beta = k * beta[..., None]
    m = jnp.einsum('bhncd,bhnsd->bhncs', k_beta, k) * decay
    m = jnp.where(tri_strict, m, 0.0) + jnp.eye(CHUNK, dtype=jnp.float32)
    rhs = jnp.concatenate([v * beta[..., None], k_beta * jnp.exp(g)[..., None]], axis=-1)
    sol = lax.linalg.triangular_solve(m, rhs, left_side=True, lower=True, unit_diagonal=True)
    u, w = sol[..., :dv], sol[..., dv:]
    attn = jnp.einsum('bhncd,bhnsd->bhncs', q, k) * decay
    g_last = g[..., -1]
    k_end = k * jnp.exp(g_last[..., None] - g)[..., None]
    q_dec = q * jnp.exp(g)[..., None]

    def step(state, xs):
        u_c, w_c, qd_c, at_c, ke_c, gl_c = xs
        v_new = u_c - jnp.einsum('bhcd,bhde->bhce', w_c, state)
        o_c = jnp.einsum('bhcd,bhde->bhce', qd_c, state) + jnp.einsum('bhcs,bhse->bhce', at_c, v_new)
        state = state * jnp.exp(gl_c)[..., None, None] + jnp.einsum('bhcd,bhce->bhde', ke_c, v_new)
        return state, o_c

    xs = tuple(jnp.moveaxis(t, 2, 0) for t in (u, w, q_dec, attn, k_end, g_last))
    s_final, o = lax.scan(step, s0, xs)
    o = jnp.moveaxis(o, 0, 2).reshape(bsz, h, n, dv)
    return o, s_final

def delta_bidirectional(lat, ctx_side):
    q, k, v, g, beta = lat
    qc, kc, vc, gc, bc = ctx_side
    s0 = jnp.zeros((q.shape[0], B_HEADS, B_DK, B_DV), jnp.float32)
    flip = lambda t: jnp.flip(t, axis=2)
    oc_f, s_f = gated_delta_chunked(qc, kc, vc, gc[0], bc[0], s0)
    o_f, _ = gated_delta_chunked(q, k, v, g[0], beta[0], s_f)
    oc_b, s_b = gated_delta_chunked(flip(qc), flip(kc), flip(vc), flip(gc[1]), flip(bc[1]), s0)
    o_b, _ = gated_delta_chunked(flip(q), flip(k), flip(v), flip(g[1]), flip(beta[1]), s_b)
    return o_f + flip(o_b), oc_f + flip(oc_b)

def delta_post(o, dn_norm_w, z):
    bsz, _, n, _ = o.shape
    o = rmsnorm(o.transpose(0, 2, 1, 3), dn_norm_w)
    zf = jax.nn.silu(z.reshape(bsz, n, B_HEADS, B_DV).astype(jnp.float32))
    return (o * zf).reshape(bsz, n, V_B).astype(z.dtype)

def hybrid_layer(x, ctx, c, c_ctx, cos, sin, lam_init, w_ada, b_ada, norm_w, w_in, conv_w,
                 a_log, dt_bias, dn_norm_w, lam_p, subln_w, w_out, update_ctx):
    mod_lat = jax.nn.silu(c) @ w_ada + b_ada
    mod_ctx = jax.nn.silu(c_ctx) @ w_ada + b_ada
    sh, sc, gt = jnp.split(mod_lat[:, None, :], 3, axis=-1)
    sh_c, sc_c, gt_c = jnp.split(mod_ctx, 3, axis=-1)
    p = (rmsnorm(x, norm_w) * (1.0 + sc) + sh) @ w_in
    pc = (rmsnorm(ctx, norm_w) * (1.0 + sc_c) + sh_c) @ w_in
    qa, ka, va, za, qkvb, zb, ab = split_in(p)
    qa_c, ka_c, va_c, za_c, qkvb_c, zb_c, ab_c = split_in(pc)

    lp = lam_p.astype(jnp.float32)
    lam = jnp.exp(jnp.sum(lp[0] * lp[1])) - jnp.exp(jnp.sum(lp[2] * lp[3])) + lam_init
    q_l = qk_heads(qa, cos, sin)
    k_l = qk_heads(ka, cos, sin)
    k_c = qk_heads(ka_c)
    v_c = v_heads(va_c)
    k_all = jnp.concatenate([k_l, k_c], axis=3)
    v_all = jnp.concatenate([v_heads(va), v_c], axis=2)
    y_a = diff_post(diff_attend_blocked(q_l, k_all, v_all, lam), subln_w, lam_init, za)

    lat_in = delta_prep(qkvb, ab, conv_w, a_log, dt_bias)
    ctx_in = delta_prep(qkvb_c, ab_c, conv_w, a_log, dt_bias)
    o_b, o_bc = delta_bidirectional(lat_in, ctx_in)
    y_b = delta_post(o_b, dn_norm_w, zb)

    x = x + gt * (jnp.concatenate([y_a, y_b], axis=-1) @ w_out)
    if update_ctx:
        y_ac = diff_post(diff_attend(qk_heads(qa_c), k_c, v_c, lam), subln_w, lam_init, za_c)
        y_bc = delta_post(o_bc, dn_norm_w, zb_c)
        ctx = ctx + gt_c * (jnp.concatenate([y_ac, y_bc], axis=-1) @ w_out)
    return x, ctx

def setup_inputs(seed: int = 0) -> dict:
    key = jax.random.key(seed)
    ks = jax.random.split(key, 16)
    f32 = jnp.float32
    nrm = lambda k, shape, s: jax.random.normal(k, shape, f32) * s
    x = nrm(ks[0], (BATCH, SEQ, D_MODEL), 1.0)
    c = nrm(ks[1], (BATCH, D_MODEL), 1.0)
    ctx = nrm(ks[2], (BATCH, CTX_LEN, D_MODEL), 1.0)
    c_ctx = nrm(ks[3], (D_MODEL,), 1.0)
    w_ada = nrm(ks[4], (DEPTH, D_MODEL, 3 * D_MODEL), 0.5 * D_MODEL ** -0.5)
    b_ada = nrm(ks[5], (DEPTH, 3 * D_MODEL), 0.02)
    norm_w = 1.0 + nrm(ks[6], (DEPTH, D_MODEL), 0.02)
    w_in = nrm(ks[7], (DEPTH, D_MODEL, N_IN), D_MODEL ** -0.5)
    conv_w = nrm(ks[8], (DEPTH, CONV_K, CONV_CH), CONV_K ** -0.5)
    dn_a_log = jnp.log(jax.random.uniform(ks[9], (DEPTH, 2, B_HEADS), f32, 1.0, 16.0))
    dt = jnp.exp(jax.random.uniform(ks[10], (DEPTH, 2, B_HEADS), f32, math.log(1e-3), math.log(1e-1)))
    dn_dt_bias = dt + jnp.log(-jnp.expm1(-dt))
    dn_norm_w = 1.0 + nrm(ks[11], (DEPTH, B_DV), 0.02)
    diff_lambda = nrm(ks[12], (DEPTH, 4, A_HEAD_DIM), 0.1)
    subln_w = 1.0 + nrm(ks[13], (DEPTH, A_VAL_DIM), 0.02)
    w_out = nrm(ks[14], (DEPTH, D_MIX, D_MODEL), D_MIX ** -0.5)
    final_norm_w = 1.0 + nrm(ks[15], (D_MODEL,), 0.02)
    return {'x': x, 'c': c, 'ctx': ctx, 'c_ctx': c_ctx, 'w_ada': w_ada, 'b_ada': b_ada,
            'norm_w': norm_w, 'w_in': w_in, 'conv_w': conv_w, 'dn_a_log': dn_a_log,
            'dn_dt_bias': dn_dt_bias, 'dn_norm_w': dn_norm_w, 'diff_lambda': diff_lambda,
            'subln_w': subln_w, 'w_out': w_out, 'final_norm_w': final_norm_w}

def reference(x, c, ctx, c_ctx, w_ada, b_ada, norm_w, w_in, conv_w, dn_a_log, dn_dt_bias,
              dn_norm_w, diff_lambda, subln_w, w_out, final_norm_w):
    n_lat = x.shape[1]
    n_rows = n_lat // GRID_W
    rows = jnp.repeat(jnp.arange(n_rows, dtype=jnp.float32), GRID_W)
    cols = jnp.tile(jnp.arange(GRID_W, dtype=jnp.float32), n_rows)
    cos, sin = axial_rope(rows, cols)
    for i in range(DEPTH):
        lam_init = 0.8 - 0.6 * math.exp(-0.3 * i)
        x, ctx = hybrid_layer(x, ctx, c, c_ctx, cos, sin, lam_init, w_ada[i], b_ada[i],
                              norm_w[i], w_in[i], conv_w[i], dn_a_log[i], dn_dt_bias[i],
                              dn_norm_w[i], diff_lambda[i], subln_w[i], w_out[i],
                              update_ctx=(i < DEPTH - 1))
    return rmsnorm(x, final_norm_w)


_drawn_inputs = setup_inputs


def setup_inputs(seed=0):
    import zlib

    import numpy as np

    out = dict(_drawn_inputs(seed))
    spreads = {}
    factors = {'norm_w': 7.831,
     'dn_norm_w': 8.0,
     'diff_lambda': 8.0,
     'subln_w': 8.0,
     'final_norm_w': 2.749}
    for name, (base, spread) in spreads.items():
        noise = np.random.default_rng([zlib.crc32(name.encode()), seed]).standard_normal(out[name].shape)
        drawn = base * np.exp(spread * noise) if base else spread * noise
        out[name] = jnp.asarray(drawn.astype(out[name].dtype))
    for name, factor in factors.items():
        out[name] = (out[name] * factor).astype(out[name].dtype)
    return out
```

```python
from contextlib import ExitStack

import numpy as np

import concourse.bass as bass
from concourse import mybir

ALU = mybir.AluOpType
ACT = mybir.ActivationFunctionType
AX = mybir.AxisListType.X
F32 = mybir.dt.float32
F32R = mybir.dt.float32r
BF16 = mybir.dt.bfloat16

P = 128
D = 2048
KT = D // P
N_CTX = 256
T = 512
NT = T // P
DEPTH = 2
HEADS = 8
GRID_W = 64
QK_A = V_A = QK_B = V_B = 1024
CONV_K = 5
N_IN = 2 * QK_A + 2 * V_A + 2 * QK_B + V_B + V_B + 4 * HEADS
HALF = KT // 2
UNIT = HALF * P
TILES = 8
UNITS = 2 * TILES
SLOTS = 4 * UNITS
PAD = CONV_K // 2
SEG = N_CTX + 2 * PAD
NORM_EPS = 1e-6
SUBLN_EPS = 1e-5
FAR = -1.0e30
LEVELS = (2, 4, 8, 16, 32, 64)

BQ, BK, BV, AK, AV, AQ, ZA, ZB = range(TILES)
BASE_B = 2 * QK_A + 2 * V_A
COLUMN = {BQ: BASE_B, BK: BASE_B + QK_B, BV: BASE_B + 2 * QK_B, AK: QK_A, AV: 2 * QK_A,
          AQ: 0, ZA: 2 * QK_A + V_A, ZB: BASE_B + 2 * QK_B + V_B}

C_ID = 0
C_TRI = C_ID + P
C_FAR = C_TRI + 2 * P
C_ONE = C_FAR + 2 * P
C_ROT = C_ONE + P
C_COS = C_ROT + P
C_SIN = C_COS + N_CTX
C_SEL = C_SIN + N_CTX
C_END = C_SEL + 2


def shape_constants():
    i = np.arange(P)
    c = np.zeros((P, C_END), np.float32)
    c[:, C_ID:C_ID + P] = np.eye(P)
    before = (i[:, None] <= i[None, :]).astype(np.float32)
    c[:, C_TRI:C_TRI + P] = before
    c[:, C_TRI + P:C_TRI + 2 * P] = before.T
    c[:, C_FAR:C_FAR + P] = (1 - before) * FAR
    c[:, C_FAR + P:C_FAR + 2 * P] = (1 - before.T) * FAR
    c[:, C_ONE:C_ONE + P] = 1.0
    half = 32
    for m in range(P):
        d = m % (2 * half)
        c[m + half if d < half else m - half, C_ROT + m] = -1.0 if d < half else 1.0
    freqs = half // 2
    inv = np.float32(10000.0) ** (-np.arange(freqs, dtype=np.float32) / np.float32(freqs))
    tok = np.arange(N_CTX)
    rows = (tok // GRID_W).astype(np.float32)
    cols = (tok % GRID_W).astype(np.float32)
    ang = np.concatenate([rows[:, None] * inv, cols[:, None] * inv], axis=-1).astype(np.float32)
    c[:, C_COS:C_COS + N_CTX] = np.cos(ang).T[i % half]
    c[:, C_SIN:C_SIN + N_CTX] = np.sin(ang).T[i % half]
    for v in range(2):
        c[:, C_SEL + v] = i % 32 == v
    m = np.zeros((P, 1 + len(LEVELS), 2, P), np.float32)
    for n, b in enumerate((1,) + LEVELS):
        blk = i // b
        low = (blk[None, :] % 2 == 0) & (blk[:, None] == blk[None, :] + 1)
        m[:, n, 0] = low
        m[:, n, 1] = low.T
    return c, m.reshape(P, -1)


class Count:

    def __init__(self, eng, sem):
        self.eng, self.sem, self.n = eng, sem, 0

    def finish(self):
        if self.n:
            self.note()
            self.settle()
            self.eng.sem_clear(self.sem)
            self.n = 0

    def done(self, ins):
        self.go(ins)
        self.eng.wait_ge(self.sem, self.n)

    def go(self, ins):
        ins.then_inc(self.sem, 1)
        self.n += 1

    def note(self):
        self.eng.sem_inc(self.sem, 1)
        self.n += 1

    def settle(self):
        self.eng.wait_ge(self.sem, self.n)


def need(eng, sem, value):
    if not isinstance(value, int) or value > 0:
        eng.wait_ge(sem, value)


def build_trunk(nc, x, c, ctx_in, c_ctx, w_ada, b_ada, norm_w, w_in, conv_w, dn_a_log, dn_dt_bias,
                dn_norm_w, diff_lambda, subln_w, w_out, final_norm_w, consts, masks, out):
    x_dram = nc.dram_tensor("x_channel_major", [KT, P, T], F32).ap()
    y_dram = nc.dram_tensor("mixed", [DEPTH, KT, P, T], F32).ap()
    g_dram = nc.dram_tensor("decay_rows", [DEPTH, 2 * HEADS, T], F32).ap()
    toks = [ctx_in.rearrange("b n d -> (b n) d"), x.rearrange("b n d -> (b n) d")]
    out2 = out.rearrange("b n d -> (b n) d")
    lam_init = [0.8 - 0.6 * float(np.exp(-0.3 * i)) for i in range(DEPTH)]

    with ExitStack() as ctx:
        def sb(name, shape, dt=F32):
            return ctx.enter_context(nc.sbuf_tensor(name, shape, dt))

        def sem(name):
            return ctx.enter_context(nc.semaphore(name))

        h_hi = sb("h_hi", [P, KT, T], F32R)
        h_lo = sb("h_lo", [P, KT, T], F32R)
        w_raw = sb("w_raw", [P, 4, HALF, P])
        w_hi = sb("w_hi", [P, 2, HALF, P], F32R)
        w_lo = sb("w_lo", [P, 2, HALF, P], F32R)
        ada_raw = sb("ada_raw", [P, 2, HALF, P])
        ada_sb = sb("ada_sb", [P, P])
        cst = sb("cst", [P, C_END])
        msk = sb("msk", [P, 1 + len(LEVELS), 2, P], BF16)
        vecs = sb("vecs", [P, 4, P])
        c_T = sb("c_T", [P, KT, 32])
        mod = sb("mod", [P, DEPTH, 3 * KT, 2])
        scale_w = sb("scale_w", [P, KT, 2])
        tab = sb("tab", [P, 5, 2, NT, HEADS])
        hcol = sb("hcol", [P, 5, 2, NT])
        convh = sb("convh", [P, CONV_K, 3])
        lam = sb("lam", [P, DEPTH])
        alog = sb("alog", [P, 2, DEPTH, 2 * HEADS])
        small = sb("small", [P, 64])
        minus_half = sb("minus_half", [P, 8])
        halfw = sb("halfw", [P, DEPTH, 2])

        arena_size = 22300
        arena = sb("arena", [P, arena_size])
        at = [0]

        def carve(n):
            at[0] += n
            assert at[0] <= arena_size, at[0]
            return arena[:, at[0] - n:at[0]]

        cin = carve(2 * SEG).rearrange("p (s n) -> p s n", s=2)
        qkv = carve(3 * T).rearrange("p (x t) -> p x t", x=3)
        th = carve(T)
        a_q, a_k, a_v = carve(T), carve(T), carve(T)
        a_raw = carve(N_CTX)
        z_a, z_b = carve(T), carve(T)
        th_z = carve(T)
        qk_tok = carve(2 * T).rearrange("p (c d) -> p c d", d=P)
        qk_T = carve(2 * T).rearrange("p (c d) -> p c d", d=P)
        v_tok = carve(T).rearrange("p (c d) -> p c d", d=P)
        k_grow = carve(2 * T).rearrange("p (x c d) -> p x c d", x=2, d=P)
        k_end = carve(2 * T).rearrange("p (x c d) -> p x c d", x=2, d=P)
        q_dec = carve(2 * T).rearrange("p (x c d) -> p x c d", x=2, d=P)
        att_T = carve(2 * T).rearrange("p (x c d) -> p x c d", x=2, d=P)
        m_T = carve(2 * T).rearrange("p (x c d) -> p x c d", x=2, d=P)
        inv = carve(2 * T).rearrange("p (x c d) -> p x c d", x=2, d=P)
        inv_T = carve(2 * T).rearrange("p (x c d) -> p x c d", x=2, d=P)
        prod = carve(2 * T).rearrange("p (x c d) -> p x c d", x=2, d=P)
        g_row = carve(2 * T).rearrange("p (x c d) -> p x c d", x=2, d=P)
        decay = carve(2 * T).rearrange("p (x c d) -> p x c d", x=2, d=P)
        va_tok = carve(T).rearrange("p (c d) -> p c d", d=P)
        prob = carve(2 * T).rearrange("p (m n) -> p m n", m=2)
        prob_T = carve(T).rearrange("p (c d) -> p c d", d=P)
        o_a = carve(T).rearrange("p (c d) -> p c d", d=P)
        y_a, y_b = carve(T), carve(T)
        w_T = inv
        states = m_T
        v_new = prod
        o_b = decay[:, 0]
        sq_b = prod.rearrange("p x c d -> p (x c) d")
        sq_a = prob
        at[0] = 0
        xT = carve(KT * T).rearrange("p (k t) -> p k t", k=KT)
        x_rms = carve(T)
        sq_tile = carve(T)
        sq_sum = carve(T)
        diag = carve(T)
        h_tmp = carve(2 * T).rearrange("p (b t) -> p b t", b=2)
        x_old = carve(2 * T).rearrange("p (b t) -> p b t", b=2)
        y_in = carve(2 * T).rearrange("p (b t) -> p b t", b=2)
        at_xin = at[0]
        x_in = carve(2 * D).rearrange("p (b n) -> p b n", b=2)
        rows_in = carve(4 * P).rearrange("p (b n) -> p b n", b=4)
        lam_in = carve(DEPTH * 4 * 64)
        N_RING = 3
        ada_ring = [w_raw[:, s] for s in range(4)] + [ada_raw[:, s] for s in range(2)]
        at[0] = at_xin
        o_row = carve(2 * D).rearrange("p (b n) -> p b n", b=2)

        ps = ctx.enter_context(nc.psum_tensor("ps", [P, 8, T], F32))
        PJ, G0, G1, G2, G3, A0, A1 = 0, 2, 3, 4, 5, 6, 7
        GX, GT = (G0, G2), (G1, G3)

        ident = cst[:, C_ID:C_ID + P]
        ones = cst[:, C_ONE:C_ONE + P]
        rot = cst[:, C_ROT:C_ROT + P]
        cos_t, sin_t = cst[:, C_COS:C_COS + N_CTX], cst[:, C_SIN:C_SIN + N_CTX]
        far = cst[:, C_FAR:C_FAR + 2 * P].rearrange("p (x d) -> p x d", x=2)
        sel = cst[:, C_SEL:C_SEL + 2]
        TAB_BETA, TAB_GROW, TAB_END, TAB_G, TAB_LAST = range(5)

        def bank(b, n=T):
            return ps[:, b, 0:n]

        def quads(b):
            return ps[:, b, :].rearrange("p (c d) -> p c d", d=P)

        rows_loaded, consts_loaded = sem("rows_loaded"), sem("consts_loaded")
        x_loaded = [sem(f"x_loaded{b}") for b in range(2)]
        setup_turned, x_turned, x_evacuated = sem("setup_turned"), sem("x_turned"), sem("x_evacuated")
        staged, c_ready, x_stored, lam_exp = sem("staged"), sem("c_ready"), sem("x_stored"), sem("lam_exp")
        masks_loaded = sem("masks_loaded")
        vec_setup = sem("vec_setup")
        w_loaded = [sem(f"w_loaded{s}") for s in range(4)]
        w_hi_ready, w_split, w_used = sem("w_hi_ready"), sem("w_split"), sem("w_used")
        ada_loaded = [sem(f"ada_loaded{s}") for s in range(6)]
        ada_used, ada_copied = sem("ada_used"), sem("ada_copied")
        ada_turned, mod_ready = sem("ada_turned"), sem("mod_ready")
        sums_ready, sums_turned, sums_copied = sem("sums_ready"), sem("sums_turned"), sem("sums_copied")
        rms_ready, diag_ready, rms_spread, rms_copied = sem("rms_ready"), sem("diag_ready"), sem("rms_spread"), sem("rms_copied")
        x_scaled, h_hi_ready, h_ready = sem("x_scaled"), sem("h_hi_ready"), sem("h_ready")
        evacuated = sem("evacuated")
        conv_done, tanh_done, qkv_ready = sem("conv_done"), sem("tanh_done"), sem("qkv_ready")
        rot_done, rope_done = sem("rot_done"), sem("rope_done")
        z_tanh, z_ready = sem("z_tanh"), sem("z_ready")
        ab_turned, ab_exp, tab_g, tab_beta, tab_sums = sem("ab_turned"), sem("ab_exp"), sem("tab_g"), sem("tab_beta"), sem("tab_sums")
        tab_ready, tab_abs, tab_soft, tab_last, tab_rows = sem("tab_ready"), sem("tab_abs"), sem("tab_soft"), sem("tab_last"), sem("tab_rows")
        rows_copied, rows_stored, g_loaded = sem("rows_copied"), sem("rows_stored"), sem("g_loaded")
        decay_arg, decay_ready = sem("decay_arg"), sem("decay_ready")
        qk_turned, v_turned, qk_squared, qk_summed, qk_rms = sem("qk_turned"), sem("v_turned"), sem("qk_squared"), sem("qk_summed"), sem("qk_rms")
        vb_ready, qk_normed, qk_returned, qk_T_ready, grams = sem("vb_ready"), sem("qk_normed"), sem("qk_returned"), sem("qk_T_ready"), sem("grams")
        k_scaled, inv_started, inv_turned, inv_copied = sem("k_scaled"), sem("inv_started"), sem("inv_turned"), sem("inv_copied")
        x_product = [sem(f"x_product{d}") for d in range(2)]
        x_masked = [sem(f"x_masked{d}") for d in range(2)]
        t_product = [sem(f"t_product{d}") for d in range(2)]
        t_merged = [sem(f"t_merged{d}") for d in range(2)]
        q_decayed, w_product, w_ready = sem("q_decayed"), sem("w_product"), sem("w_ready")
        v_product, v_ready, s_product, s_ready = sem("v_product"), sem("v_ready"), sem("s_product"), sem("s_ready")
        ob_product, ob_squared, ob_summed, ob_rms, ob_normed = sem("ob_product"), sem("ob_squared"), sem("ob_summed"), sem("ob_rms"), sem("ob_normed")
        ob_turned, yb_ready, yb_stored = sem("ob_turned"), sem("yb_ready"), sem("yb_stored")
        va_turned, va_ready, scored, maxed, exped, mixed = sem("va_turned"), sem("va_ready"), sem("scored"), sem("maxed"), sem("exped"), sem("mixed")
        p_turned, p_copied, oa_product, oa_copied = sem("p_turned"), sem("p_copied"), sem("oa_product"), sem("oa_copied")
        oa_squared, oa_summed, oa_rms, oa_normed = sem("oa_squared"), sem("oa_summed"), sem("oa_rms"), sem("oa_normed")
        oa_turned, ya_ready, ya_stored = sem("oa_turned"), sem("ya_ready"), sem("ya_stored")
        y_loaded = [sem(f"y_loaded{b}") for b in range(2)]
        y_hi_ready, y_split, out_added = sem("y_hi_ready"), sem("y_split"), sem("out_added")
        old_loaded = [sem(f"old_loaded{b}") for b in range(2)]
        x_squared, x_scratch = sem("x_squared"), sem("x_scratch")
        fin_scaled, fin_turned, fin_copied, fin_stored = sem("fin_scaled"), sem("fin_turned"), sem("fin_copied"), sem("fin_stored")
        vec_step, act_step, sp_step, pool_step = sem("vec_step"), sem("act_step"), sem("sp_step"), sem("pool_step")

        def first_q(layer):
            return 0 if layer < DEPTH - 1 else N_CTX // P

        def tokens(layer, tile):
            return 0 if tile in (BK, BV, AK, AV) else first_q(layer) * P

        LAYER_UNITS = 2 + HEADS * UNITS + 2 * KT
        ALL_UNITS = DEPTH * LAYER_UNITS
        LAYER_TILES = 1 + HEADS * TILES
        ADA_START = 2 * KT
        ADA_IN = {0: 6, 1: 2}

        def ada_block(layer, k):
            return [(0, 2 * KT), (1, 0), (1, KT)][k // 2] if layer == 0 else (1, 2 * KT)

        def ada_before(layer):
            return ADA_START + (0 if layer == 0 else HEADS * ADA_IN[0])

        def nth(layer, i, off, per=1, idx=1):
            return i * per + (HEADS * layer + off) * per + idx

        LVL = len(LEVELS)
        q_tiles = {0: (2, 3, 0, 1), 1: (2, 3)}
        QT_BEFORE = {0: 0, 1: HEADS * 4}

        def nth_q(layer, i, off, idx):
            per = len(q_tiles[layer])
            return i * per + (QT_BEFORE[layer] + off * per + idx)

        ORDER = ((0, 1, 2, 3), (1, 0, 3, 2))

        block = ctx.enter_context(nc.Block())

        def heads(eng, layer, body):
            body(0, True, False)
            if layer == 0:
                body(1, True, True)
            with eng.Fori(2 if layer == 0 else 1, HEADS) as i:
                body(i, True, True)
            body(HEADS, False, True)

        @block.sync
        def _(sp):
            sp.dma_start(cst[:], consts).then_inc(consts_loaded, 16)
            sp.wait_ge(staged, 1)
            sp.dma_start(rows_in[0:16, 0], c_ctx.rearrange("(k p) -> k p", p=P)).then_inc(rows_loaded, 16)
            sp.dma_start(rows_in[16:32, 0], c.rearrange("b (k p) -> (b k) p", p=P)).then_inc(rows_loaded, 16)
            sp.dma_start(rows_in[32:64, 0], norm_w.rearrange("l (k p) -> (l k) p", p=P)).then_inc(rows_loaded, 16)
            sp.dma_start(rows_in[64:80, 0], final_norm_w.rearrange("(k p) -> k p", p=P)).then_inc(rows_loaded, 16)
            sp.dma_start(rows_in[80:82, 0], dn_norm_w).then_inc(rows_loaded, 16)
            sp.dma_start(rows_in[82:84, 0], subln_w).then_inc(rows_loaded, 16)
            sp.dma_start(rows_in[0:96, 1], b_ada.rearrange("l (k p) -> (l k) p", p=P)).then_inc(rows_loaded, 16)
            for l in range(DEPTH):
                sp.dma_start(rows_in[0:120, 2 + l],
                             conv_w[l].rearrange("j (k p) -> (j k) p", p=P)).then_inc(rows_loaded, 16)
            sp.dma_start(lam_in, diff_lambda.rearrange("l a d -> (l a d)").unsqueeze(0)
                         .to_broadcast([P, DEPTH * 4 * 64])).then_inc(rows_loaded, 16)
            for n, v in enumerate((dn_a_log, dn_dt_bias)):
                sp.dma_start(alog[:, n].rearrange("p l h -> p (l h)"),
                             v.rearrange("l a h -> (l a h)").unsqueeze(0)
                             .to_broadcast([P, DEPTH * 2 * HEADS])).then_inc(rows_loaded, 16)

            def load_x(n):
                if n >= 2:
                    sp.wait_ge(x_turned, (n - 1) * 4)
                sp.dma_start(x_in[:, n % 2], toks[n // 2][(n % 2) * P:(n % 2 + 1) * P, :]).then_inc(x_loaded[n % 2], 16)

            def ada_columns(layer, block_, half):
                return w_ada[layer].rearrange("(k p) n -> p k n", p=P)[:, half * HALF:(half + 1) * HALF,
                                                                      bass.ds(block_ * P, P)]

            ring = 6
            for u in range(2 * ADA_START):
                if u in (0, 4, 8, 12):
                    load_x(u // 4)
                if u >= ring:
                    sp.wait_ge(ada_used, u - ring + 1)
                sp.dma_start(ada_ring[u % ring], ada_columns(0, u // 2, u % 2)).then_inc(ada_loaded[u % ring], 16)

            def w_unit(i, u, source):
                s = u % 4
                if isinstance(i, int) and i * UNITS + u < 4:
                    sp.wait_ge(ada_used, 2 * ADA_START)
                else:
                    sp.wait_ge(w_split, i * UNITS + (u - 3))
                    sp.sem_inc(sp_step, 1)
                sp.dma_start(w_raw[:, s], source).then_inc(w_loaded[s], 16)

            def ada_unit(layer, i, k, half):
                lay, first = ada_block(layer, k)
                n = i * (2 * ADA_IN[layer]) + (ada_before(layer) * 2 + 2 * k + half)
                sp.wait_ge(ada_used, n - 1)
                sp.sem_inc(sp_step, 1)
                sp.dma_start(ada_raw[:, half], ada_columns(lay, i * 2 + (first + k % 2), half)).then_inc(
                    ada_loaded[4 + half], 16)

            for layer in range(DEPTH):
                base = layer * LAYER_UNITS
                w_cols = w_in[layer].rearrange("(k p) n -> p k n", p=P)
                for half in range(2):
                    w_unit(0, base + half, w_cols[:, half * HALF:(half + 1) * HALF, N_IN - P:N_IN])

                def body(i, project, fill):
                    if not project:
                        return
                    for k in range(UNITS):
                        t, half = k // 2, k % 2
                        w_unit(i, base + 2 + k,
                               w_cols[:, half * HALF:(half + 1) * HALF, bass.ds(i * P + COLUMN[t], P)])
                        if k >= 10 and k - 10 < ADA_IN[layer]:
                            for hf in range(2):
                                ada_unit(layer, i, k - 10, hf)
                heads(sp, layer, body)
                wo = w_out[layer].rearrange("(k p) n -> p k n", p=P)
                for n in range(KT):
                    for half in range(2):
                        u = base + 2 + HEADS * UNITS + 2 * n + half
                        w_unit(0, u, wo[:, half * HALF:(half + 1) * HALF, n * P:(n + 1) * P])

        @block.scalar
        def _(act):
            own = Count(act, act_step)

            def split_hi(i, u):
                s = u % 4
                act.wait_ge(w_loaded[s], i * (16 * UNITS // 4) + 16 * (u // 4 + 1))
                need(act, w_used, i * UNITS + (u - 1))
                nc.scalar.copy(w_hi[:, u % 2], w_raw[:, s]).then_inc(w_hi_ready, 1)

            act.wait_ge(setup_turned, 1)
            own.done(nc.scalar.copy(vecs[:].rearrange("p b n -> p (b n)"), bank(A0)))
            nc.scalar.activation(small[:, 0:2 * KT], vecs[:, 0, 0:2 * KT], ACT.Tanh, scale=0.5).then_inc(c_ready, 1)
            act.wait_ge(c_ready, 1)
            act.wait_ge(staged, 3)
            nc.scalar.activation(small[:, 40:44], small[:, 40:44], ACT.Exp).then_inc(lam_exp, 1)

            def copy_x(n, q):
                act.wait_ge(x_turned, n * 4 + q + 1)
                nc.scalar.copy(xT[:, 4 * q:4 * q + 4, n * P:(n + 1) * P], quads(G0 + q)).then_inc(x_evacuated, 1)
                act.wait_ge(x_evacuated, n * 4 + q + 1)

            def ada_copy(value):
                act.wait_ge(ada_used, value * 2)
                need(act, ada_turned, value - 1)
                nc.scalar.copy(ada_sb[:], bank(A0, P)).then_inc(ada_copied, 1)
                act.wait_ge(ada_copied, value)

            for b in range(ADA_START):
                if b % 4 == 2 and b // 4 < NT:
                    for q in range(4):
                        copy_x(b // 4, q)
                ada_copy(b + 1)

            for k in range(KT):
                if k >= 1:
                    act.wait_ge(vec_setup, k)
                nc.scalar.activation(sq_tile, xT[:, k], ACT.Square).then_inc(x_squared, 1)
                act.wait_ge(x_squared, k + 1)
            act.dma_start(x_dram.rearrange("k p t -> p k t"), xT).then_inc(x_stored, 16)

            def modulate(layer):
                act.wait_ge(rms_spread, layer + 1)
                nc.scalar.copy(x_rms, bank(A1)).then_inc(rms_copied, 1)
                act.wait_ge(rms_copied, layer + 1)
                for k in range(KT):
                    act.wait_ge(x_scaled, layer * KT + k + 1)
                    if k >= 2:
                        act.wait_ge(h_ready, layer * KT + k - 1)
                    for v in range(2):
                        seg = slice(v * N_CTX, (v + 1) * N_CTX)
                        own.go(nc.scalar.activation(h_tmp[:, k % 2, seg], xT[:, k, seg], ACT.Identity,
                                                    scale=scale_w[:, k, v:v + 1], bias=mod[:, layer, k, v:v + 1]))
                    own.settle()
                    nc.scalar.copy(h_hi[:, k], h_tmp[:, k % 2]).then_inc(h_hi_ready, 1)
                    act.wait_ge(h_hi_ready, layer * KT + k + 1)

            for layer in range(DEPTH):
                base = layer * LAYER_UNITS
                c0 = first_q(layer)
                own.finish()
                split_hi(0, base)
                modulate(layer)
                split_hi(0, base + 1)
                split_hi(0, base + 2)

                def tile_count(i, off, t):
                    return i * TILES + (layer * LAYER_TILES + 1 + off * TILES + t + 1)

                act.wait_ge(w_used, base + 2)
                nc.scalar.copy(th[96:128], ps[96:128, PJ + 0, :]).then_inc(evacuated, 1)
                act.wait_ge(evacuated, layer * LAYER_TILES + 1)

                def table_step(s):
                    gx = decay[:, 0, 0, 0:NT * 16].rearrange("p (c n) -> p c n", c=NT)
                    e = decay[:, 0, 1, 0:NT * 16].rearrange("p (c n) -> p c n", c=NT)
                    tb = decay[:, 0, 2, 0:NT * 16].rearrange("p (c n) -> p c n", c=NT)
                    raw = bank(A0, P).rearrange("p (c n) -> p c n", c=NT)
                    if s == 0:
                        act.wait_ge(tab_g, layer + 1)
                        own.done(nc.scalar.activation(e, gx, ACT.Abs))
                        own.done(nc.scalar.activation(tb, raw[:, :, 16:32], ACT.Tanh, scale=0.5))
                        own.done(nc.scalar.activation(small[:, 48:64], alog[:, 0, layer], ACT.Exp))
                        own.done(nc.scalar.activation(e, e, ACT.Exp, scale=-1.0))
                        nc.scalar.activation(e, e, ACT.Ln, bias=1.0).then_inc(tab_soft, 1)
                        act.wait_ge(tab_soft, layer + 1)
                    if s == 1:
                        act.wait_ge(tab_last, layer + 1)
                        tabf = tab[:].rearrange("p k x c h -> p k (x c h)")
                        own.go(nc.scalar.activation(tabf[:, TAB_GROW], bank(A1, 64), ACT.Exp))
                        own.go(nc.scalar.activation(tabf[:, TAB_LAST], ps[:, A1, 64:128], ACT.Exp))
                        nc.scalar.activation(tabf[:, TAB_END], decay[:, 0, 3, 0:64], ACT.Exp).then_inc(tab_ready, 1)
                        act.wait_ge(tab_ready, layer + 1)
                        own.settle()
                    if s == 2:
                        act.wait_ge(tab_rows, layer + 1)
                        nc.scalar.copy(sq_b[0:16, 0:4, :].rearrange("p c d -> p (c d)"), ps[0:16, A0, :]).then_inc(rows_copied, 1)
                        act.wait_ge(rows_copied, layer + 1)
                        act.dma_start(g_dram[layer], sq_b[0:16, 0:4, :].rearrange("p c d -> p (c d)")).then_inc(rows_stored, 16)
                        act.wait_ge(rows_stored, 16 * (layer + 1))

                def load_g(i, off):
                    rows = g_dram[layer].rearrange("(x h) t -> x h t", h=HEADS)[:, bass.ds(i + off, 1), :]
                    act.dma_start(g_row.rearrange("p x c d -> p x (c d)"),
                                  rows.rearrange("x o t -> o x t").to_broadcast([P, 2, T])).then_inc(g_loaded, 16)

                def body(i, project, fill):
                    own.finish()

                    def h(off=-1, per=1, idx=1):
                        return nth(layer, i, off, per, idx)

                    def evacuate(t):
                        src = bank(PJ + (1 + t) % 2)
                        q0 = tokens(layer, t)
                        act.wait_ge(w_used, i * UNITS + (base + 2 + 2 * t + 2))
                        val = tile_count(i, 0, t)
                        if t in (BQ, BK, BV):
                            need(act, conv_done, nth(layer, i, 0, 3, t))
                            s0 = q0 // N_CTX
                            nc.scalar.copy(cin[:, s0:, PAD:PAD + N_CTX],
                                           src.rearrange("p (s n) -> p s n", s=2)[:, s0:]).then_inc(evacuated, 1)
                        elif t in (AK, AQ):
                            need(act, scored, nth_q(layer, i, 0, 0))
                            need(act, rope_done, nth(layer, i, 0, 2, 0 if t == AK else 1))
                            if q0 == 0:
                                own.go(nc.scalar.copy((a_k if t == AK else a_q)[:, 0:N_CTX], src[:, 0:N_CTX]))
                            nc.scalar.copy(a_raw, src[:, N_CTX:T]).then_inc(evacuated, 1)
                            own.settle()
                        elif t == AV:
                            need(act, va_turned, h(-1))
                            nc.scalar.copy(a_v, src).then_inc(evacuated, 1)
                        act.wait_ge(evacuated, val)

                    def evacuate_z(off, t):
                        src = bank(PJ + (1 + t) % 2)
                        z = z_a if t == ZA else z_b
                        q0 = tokens(layer, t)
                        act.wait_ge(w_used, i * UNITS + (base + 2 + off * UNITS + 2 * t + 2))
                        if t == ZA:
                            need(act, ya_ready, nth(layer, i, off, 1, 0))
                            need(act, z_ready, nth(layer, i, off, 2, 0))
                        else:
                            need(act, yb_ready, nth(layer, i, off, 1, 0))
                            act.wait_ge(z_ready, nth(layer, i, off, 2, 1))
                        own.go(nc.scalar.activation(th_z[:, q0:], src[:, q0:], ACT.Tanh, scale=0.5))
                        nc.scalar.copy(z[:, q0:], src[:, q0:]).then_inc(evacuated, 1)
                        own.settle()
                        act.wait_ge(evacuated, tile_count(i, off, t))

                    def tanh(x_):
                        act.wait_ge(conv_done, nth(layer, i, 0, 3, x_ + 1))
                        q0 = tokens(layer, x_)
                        nc.scalar.activation(th[:, q0:], qkv[:, x_, q0:], ACT.Tanh, scale=0.5).then_inc(tanh_done, 1)
                        act.wait_ge(tanh_done, nth(layer, i, 0, 3, x_ + 1))

                    def squares():
                        act.wait_ge(qk_turned, h())
                        flat = ps[:, G0:G0 + 2, :].rearrange("p b (c d) -> p (b c) d", d=P)
                        nc.scalar.activation(sq_b[:, c0:], flat[:, c0:], ACT.Square).then_inc(qk_squared, 1)
                        act.wait_ge(qk_squared, h())

                    def v_copy():
                        act.wait_ge(v_turned, h())
                        nc.scalar.activation(v_tok.rearrange("p c d -> p (c d)"), bank(G2), ACT.Copy, scale=0.5).then_inc(vb_ready, 1)
                        act.wait_ge(vb_ready, h())

                    def decays():
                        act.wait_ge(decay_arg, h())
                        need(act, ob_turned, h(-2))
                        own.go(nc.scalar.activation(q_dec[:, :, c0:], g_row[:, :, c0:], ACT.Exp))
                        nc.scalar.activation(decay, decay, ACT.Exp).then_inc(decay_ready, 1)
                        act.wait_ge(decay_ready, h())
                        own.settle()
                        if not (isinstance(i, int) and i == HEADS):
                            load_g(i, 0)

                    def qk_copy():
                        act.wait_ge(qk_returned, h())
                        flat = ps[:, G0:G0 + 2, :].rearrange("p b (c d) -> p (b c) d", d=P)
                        nc.scalar.copy(qk_T[:, c0:], flat[:, c0:]).then_inc(qk_T_ready, 1)
                        act.wait_ge(qk_T_ready, h())

                    def inv_copy(d):
                        act.wait_ge(inv_turned, h(-1, 2, d + 1))
                        nc.scalar.copy(inv[:, d], quads(GT[d])).then_inc(inv_copied, 1)
                        act.wait_ge(inv_copied, h(-1, 2, d + 1))

                    def w_copy(d):
                        act.wait_ge(w_product, h(-1, 2, d + 1))
                        nc.scalar.activation(w_T[:, d], quads(GX[d]), ACT.Copy, scale=-1.0).then_inc(w_ready, 1)
                        act.wait_ge(w_ready, h(-1, 2, d + 1))

                    def v_new_copy(j):
                        act.wait_ge(v_product, h(-1, 4, j + 1))
                        for d in range(2):
                            ch = ORDER[d][j]
                            m = nc.scalar.activation(v_new[:, d, ch], ps[:, GT[d], 0:P], ACT.Copy,
                                                     scale=hcol[:, TAB_BETA, d, ch:ch + 1])
                            if d == 0:
                                own.go(m)
                        m.then_inc(v_ready, 1)
                        own.settle()
                        act.wait_ge(v_ready, h(-1, 4, j + 1))

                    def o_squares():
                        act.wait_ge(ob_product, h())
                        nc.scalar.activation(sq_b[:, c0:NT], quads(G0)[:, c0:], ACT.Square).then_inc(ob_squared, 1)
                        act.wait_ge(ob_squared, h())

                    def y_store(which):
                        yy, ready, stored = ((y_a, ya_ready, ya_stored), (y_b, yb_ready, yb_stored))[which]
                        act.wait_ge(ready, h())
                        act.dma_start(y_dram[layer][bass.ds(i + (HEADS * which - 1), 1), :, c0 * P:].rearrange("o p t -> (o p) t"),
                                      yy[:, c0 * P:]).then_inc(stored, 16)

                    def va_copy():
                        act.wait_ge(va_turned, h())
                        nc.scalar.copy(va_tok, quads(A0)).then_inc(va_ready, 1)
                        act.wait_ge(va_ready, h())

                    def exps(n):
                        qt = q_tiles[layer][n]
                        keys = T if qt >= 2 else N_CTX
                        act.wait_ge(maxed, nth_q(layer, i, -1, n + 1))
                        for m in range(2):
                            last = nc.scalar.activation(prob[:, m, 0:keys], bank(A0 + m, keys), ACT.Exp, scale=0.125,
                                                        bias=small[:, 34 + m:35 + m], accum_out=small[:, 36 + m:37 + m])
                            if m == 0:
                                own.go(last)
                        last.then_inc(exped, 1)
                        own.settle()
                        act.wait_ge(exped, nth_q(layer, i, -1, n + 1))

                    def p_copy(n):
                        qt = q_tiles[layer][n]
                        kt = NT if qt >= 2 else 2
                        act.wait_ge(p_turned, nth_q(layer, i, -1, n + 1))
                        nc.scalar.copy(prob_T[:, 0:kt], quads(A0)[:, 0:kt]).then_inc(p_copied, 1)
                        act.wait_ge(p_copied, nth_q(layer, i, -1, n + 1))

                    def oa_copy(n):
                        act.wait_ge(oa_product, nth_q(layer, i, -1, n + 1))
                        nc.scalar.copy(o_a[:, q_tiles[layer][n]], bank(A1, P)).then_inc(oa_copied, 1)
                        act.wait_ge(oa_copied, nth_q(layer, i, -1, n + 1))

                    def oa_squares():
                        nc.scalar.activation(sq_a[:, 0, c0 * P:], o_a[:, c0:].rearrange("p c d -> p (c d)"),
                                             ACT.Square).then_inc(oa_squared, 1)
                        act.wait_ge(oa_squared, h())

                    def ada(k):
                        ada_copy(i * ADA_IN[layer] + (ada_before(layer) + k + 1))

                    plan = {}

                    def put(s, f, *a):
                        plan.setdefault(s, []).append((f, a))

                    if fill:
                        put(0, evacuate_z, -1, ZB)
                        put(0, va_copy)
                        put(1, squares)
                        put(1, v_copy)
                        put(3, decays)
                        put(6, qk_copy)
                        put(13, inv_copy, 0)
                        put(14, inv_copy, 1)
                        put(39, w_copy, 0)
                        put(40, w_copy, 1)
                        for j in range(4):
                            put(42 + 4 * j, v_new_copy, j)
                        put(57, o_squares)
                        put(62, y_store, 1)
                        for n in range(len(q_tiles[layer])):
                            put(3 + 8 * n, exps, n)
                            put(7 + 8 * n, p_copy, n)
                            put(9 + 8 * n, oa_copy, n)
                        put(3 + 8 * len(q_tiles[layer]), oa_squares)
                        put(39, y_store, 0)
                    if project:
                        for t in (BQ, BK, BV, AK, AV, AQ):
                            put(8 * t + 8, evacuate, t)
                        for x_ in range(3):
                            put(8 * x_ + 14, tanh, x_)
                        put(56, evacuate_z, 0, ZA)
                        for k in range(ADA_IN[layer]):
                            put(43 + 3 * k, ada, k)
                        if isinstance(i, int) and i == 0:
                            put(3, table_step, 0)
                            put(6, table_step, 1)
                            put(8, table_step, 2)
                            put(12, load_g, 0, 0)
                    for s in range(SLOTS):
                        if project and s % 4 == 0:
                            split_hi(i, base + 2 + s // 4 + 1)
                        for f, a in plan.get(s, ()):
                            f(*a)
                    own.finish()

                own.finish()
                heads(act, layer, body)

                own.finish()
                first = base + 2 + HEADS * UNITS
                for k in range(KT):
                    act.wait_ge(y_loaded[k % 2], 16 * (layer * HEADS + k // 2 + 1))
                    nc.scalar.copy(h_hi[:, k, c0 * P:], y_in[:, k % 2, c0 * P:]).then_inc(y_hi_ready, 1)
                    act.wait_ge(y_hi_ready, layer * KT + k + 1)
                for n in range(KT):
                    for half in range(2):
                        u = first + 2 * n + half + 1
                        if half == 0 or n < KT - 1:
                            split_hi(0, u)
                    act.wait_ge(out_added, layer * KT + n + 1)
                    need(act, sums_ready, layer * KT + n)
                    nc.scalar.activation(sq_tile[:, c0 * P:], xT[:, n, c0 * P:], ACT.Square).then_inc(x_squared, 1)
                    act.wait_ge(x_squared, (layer + 1) * KT + n + 1)
                    if layer == 0:
                        act.dma_start(x_dram[n, :, N_CTX:], xT[:, n, N_CTX:]).then_inc(x_stored, 16)

            act.wait_ge(rms_spread, DEPTH + 1)
            nc.scalar.copy(x_rms[:, N_CTX:], ps[:, A1, N_CTX:]).then_inc(rms_copied, 1)
            act.wait_ge(rms_copied, DEPTH + 1)
            for n in range(2):
                for q in range(4):
                    act.wait_ge(fin_turned, n * 4 + q + 1)
                    nc.scalar.copy(o_row[:, n, q * T:(q + 1) * T], bank(G0 + q)).then_inc(fin_copied, 1)
                    act.wait_ge(fin_copied, n * 4 + q + 1)
                act.dma_start(out2[n * P:(n + 1) * P, :], o_row[:, n]).then_inc(fin_stored, 16)
            act.wait_ge(fin_stored, 32)
            act.wait_ge(x_stored, 16 * (1 + KT))
            act.wait_ge(ya_stored, 16 * DEPTH * HEADS)
            act.wait_ge(yb_stored, 16 * DEPTH * HEADS)

        @block.vector
        def _(vec):
            own = Count(vec, vec_step)
            V = nc.vector

            def tt(o, a, b, op):
                return V.tensor_tensor(o, a, b, op)

            own.go(V.memset(rows_in, 0.0))
            own.go(V.memset(c_T[:], 0.0))
            own.go(V.memset(minus_half[:], -0.5))
            V.memset(sq_sum, 0.0).then_inc(staged, 1)
            vec.wait_ge(staged, 1)
            own.settle()
            vec.wait_ge(masks_loaded, 16)
            vec.wait_ge(consts_loaded, 16)
            vec.wait_ge(c_ready, 1)
            own.done(V.tensor_scalar(small[:, 0:2 * KT], small[:, 0:2 * KT], 1.0, 0.5, ALU.add, ALU.mult))
            tt(c_T[:, :, 0:2].rearrange("p k v -> p v k"), small[:, 0:2 * KT].rearrange("p (v k) -> p v k", v=2),
               vecs[:, 0, 0:2 * KT].rearrange("p (v k) -> p v k", v=2), ALU.mult).then_inc(staged, 1)
            vec.wait_ge(staged, 2)
            vec.wait_ge(rows_loaded, 16 * 12)
            lv = lam_in.rearrange("p (l a d) -> p l a d", l=DEPTH, a=4)
            own.done(tt(lv[:, :, 0::2, :], lv[:, :, 0::2, :], lv[:, :, 1::2, :], ALU.mult))
            V.tensor_reduce(small[:, 40:44].rearrange("p (l a) -> p l a", l=DEPTH), lv[:, :, 0::2, :], AX, ALU.add).then_inc(staged, 1)
            vec.wait_ge(staged, 3)

            def mod_column(value, lay, blk):
                vec.wait_ge(ada_turned, value)
                tt(mod[:, lay, bass.ds(blk, 1), :].rearrange("p o v -> p (o v)"), bank(A1, 2),
                   vecs[:, 1, bass.ds(blk + lay * 3 * KT, 1)].to_broadcast([P, 2]), ALU.add).then_inc(mod_ready, 1)
                vec.wait_ge(mod_ready, value)

            for b in range(ADA_START):
                mod_column(b + 1, 0, b)
                if b == 0:
                    for l in range(DEPTH):
                        own.done(V.tensor_scalar(halfw[:, l, 0:1], vecs[:, 0, 82 + l:83 + l], 0.5 * (1.0 - lam_init[l]), None, ALU.mult))
                        own.done(V.tensor_scalar(halfw[:, l, 1:2], vecs[:, 0, 80 + l:81 + l], 0.5, None, ALU.mult))
            for k in range(KT):
                vec.wait_ge(x_squared, k + 1)
                tt(sq_sum, sq_sum, sq_tile, ALU.add).then_inc(vec_setup, 1)
                vec.wait_ge(vec_setup, k + 1)
            vec.wait_ge(lam_exp, 1)
            for l in range(DEPTH):
                own.done(tt(lam[:, l:l + 1], small[:, 41 + 2 * l:42 + 2 * l], small[:, 40 + 2 * l:41 + 2 * l], ALU.subtract))
                own.done(V.tensor_scalar(lam[:, l:l + 1], lam[:, l:l + 1], -lam_init[l], None, ALU.add))

            def rms(n, c0):
                vec.wait_ge(sums_turned, n + 1)
                V.tensor_copy(small[:, 44 + c0:48], ps[:, A0, c0:NT]).then_inc(sums_copied, 1)
                vec.wait_ge(sums_copied, n + 1)
                vec.wait_ge(rms_ready, n + 1)
                for cc in range(c0, NT):
                    m = V.tensor_scalar(diag[:, cc * P:(cc + 1) * P], ident, small[:, 44 + cc:45 + cc], None, ALU.mult)
                    if cc < NT - 1:
                        own.go(m)
                m.then_inc(diag_ready, 1)
                vec.wait_ge(diag_ready, n + 1)
                own.settle()

            def split_lo(i, u):
                vec.wait_ge(w_hi_ready, i * UNITS + (u + 1))
                need(vec, w_used, i * UNITS + (u - 1))
                tt(w_lo[:, u % 2], w_raw[:, u % 4], w_hi[:, u % 2].bitcast(F32), ALU.subtract).then_inc(w_split, 1)

            for layer in range(DEPTH):
                base = layer * LAYER_UNITS
                c0 = first_q(layer)
                own.finish()
                split_lo(0, base)
                rms(layer, 0)
                own.done(V.scalar_tensor_tensor(
                    scale_w[:], mod[:, layer, KT:2 * KT, :], 1.0,
                    vecs[:, 0, 32 + 16 * layer:48 + 16 * layer].unsqueeze(2).to_broadcast([P, KT, 2]), ALU.add, ALU.mult))
                vec.wait_ge(rms_copied, layer + 1)
                vec.wait_ge(x_stored, 16 * (1 + layer * KT))

                def h_lo_tile(k):
                    vec.wait_ge(h_hi_ready, layer * KT + k + 1)
                    tt(h_lo[:, k], h_tmp[:, k % 2], h_hi[:, k].bitcast(F32), ALU.subtract).then_inc(h_ready, 1)
                    vec.wait_ge(h_ready, layer * KT + k + 1)

                for k in range(KT):
                    tt(xT[:, k], xT[:, k], x_rms, ALU.mult).then_inc(x_scaled, 1)
                    vec.wait_ge(x_scaled, layer * KT + k + 1)
                    if k >= 1:
                        h_lo_tile(k - 1)
                h_lo_tile(KT - 1)
                own.done(V.memset(cin, 0.0))
                split_lo(0, base + 1)

                def table_step(s):
                    gx = decay[:, 0, 0, 0:NT * 16].rearrange("p (c n) -> p c n", c=NT)
                    e = decay[:, 0, 1, 0:NT * 16].rearrange("p (c n) -> p c n", c=NT)
                    tb = decay[:, 0, 2, 0:NT * 16].rearrange("p (c n) -> p c n", c=NT)
                    raw = bank(A0, P).rearrange("p (c n) -> p c n", c=NT)
                    if s == 0:
                        vec.wait_ge(ab_turned, layer + 1)
                        tt(gx, raw[:, :, 0:16], alog[:, 1, layer].unsqueeze(1).to_broadcast([P, NT, 16]),
                           ALU.add).then_inc(tab_g, 1)
                        vec.wait_ge(tab_g, layer + 1)
                    if s == 1:
                        vec.wait_ge(tab_soft, layer + 1)
                        own.done(V.scalar_tensor_tensor(gx, gx, 0.0, e, ALU.max, ALU.add))
                        own.done(tt(gx, gx, small[:, 48:64].unsqueeze(1).to_broadcast([P, NT, 16]), ALU.mult))
                        own.done(V.tensor_scalar(tab[:, TAB_BETA].rearrange("p x c h -> p c x h"),
                                                 tb.rearrange("p c (x h) -> p c x h", x=2), 0.5, 0.5, ALU.mult, ALU.add))
                        V.tensor_scalar(gx, gx, -1.0, None, ALU.mult).then_inc(tab_beta, 1)
                        vec.wait_ge(tab_beta, layer + 1)
                    if s == 2:
                        vec.wait_ge(tab_sums, layer + 1)
                        tabf = tab[:].rearrange("p k x c h -> p k (x c h)")
                        own.done(V.tensor_copy(tabf[:, TAB_G], bank(A1, 64)))
                        own.done(V.tensor_copy(decay[:, 0, 1, 0:64].rearrange("p (c x h) -> p c x h", c=NT, x=2),
                                               tab[:, TAB_G].rearrange("p x c h -> p c x h")))
                        tt(decay[:, 0, 3, 0:64], ps[:, A1, 64:128], tabf[:, TAB_G], ALU.subtract).then_inc(tab_last, 1)
                        vec.wait_ge(tab_last, layer + 1)

                def body(i, project, fill):
                    own.finish()

                    def h(off=-1, per=1, idx=1):
                        return nth(layer, i, off, per, idx)

                    def tap(x_, j):
                        t = (BQ, BK, BV)[x_]
                        s0 = tokens(layer, t) // N_CTX
                        acc = qkv[:, x_].rearrange("p (s n) -> p s n", s=2)[:, s0:]
                        if j == 0 and x_ == 0:
                            own.done(V.tensor_copy(convh[:], vecs[:, 2 + layer, 0:CONV_K * 24].rearrange(
                                "p (j x h) -> p j x h", j=CONV_K, x=3)[:, :, :, bass.ds(i, 1)].rearrange("p j x o -> p j (x o)")))
                            need(vec, v_turned, h())
                        src = cin[:, s0:, j:j + N_CTX]
                        w = convh[:, j, x_:x_ + 1]
                        if j == 0:
                            vec.wait_ge(evacuated, i * TILES + (layer * LAYER_TILES + 1 + t + 1))
                            own.done(V.tensor_scalar(acc, src, w, None, ALU.mult))
                        else:
                            m = V.scalar_tensor_tensor(acc, src, w, acc, ALU.mult, ALU.add)
                            if j == CONV_K - 1:
                                m.then_inc(conv_done, 1)
                                vec.wait_ge(conv_done, nth(layer, i, 0, 3, x_ + 1))
                            else:
                                own.done(m)

                    def silu(x_):
                        q0 = tokens(layer, x_)
                        vec.wait_ge(tanh_done, nth(layer, i, 0, 3, x_ + 1))
                        V.scalar_tensor_tensor(qkv[:, x_, q0:], th[:, q0:], 1.0, qkv[:, x_, q0:], ALU.add,
                                               ALU.mult).then_inc(qkv_ready, 1)
                        vec.wait_ge(qkv_ready, nth(layer, i, 0, 3, x_ + 1))

                    def rope(n):
                        dst = (a_k, a_q)[n]
                        vec.wait_ge(rot_done, nth(layer, i, 0, 2, n + 1))
                        need(vec, scored, nth_q(layer, i, 0, 0))
                        lat = dst[:, N_CTX:T]
                        own.done(tt(lat, bank(A0, N_CTX), sin_t, ALU.mult))
                        own.done(tt(a_raw, a_raw, cos_t, ALU.mult))
                        tt(lat, lat, a_raw, ALU.add).then_inc(rope_done, 1)
                        vec.wait_ge(rope_done, nth(layer, i, 0, 2, n + 1))

                    def z_silu(off, n):
                        z = (z_a, z_b)[n]
                        q0 = c0 * P
                        vec.wait_ge(evacuated, i * TILES + (layer * LAYER_TILES + 1 + off * TILES + ZA + n + 1))
                        V.scalar_tensor_tensor(z[:, q0:], th_z[:, q0:], 1.0, z[:, q0:], ALU.add, ALU.mult).then_inc(z_ready, 1)
                        vec.wait_ge(z_ready, nth(layer, i, off, 2, n + 1))

                    def decay_args():
                        own.done(V.tensor_copy(hcol[:].rearrange("p k x c -> p (k x c)"),
                                               tab[:].rearrange("p k x c h -> p (k x c) h")[:, :, bass.ds(i - 1, 1)]
                                               .rearrange("p n o -> p (n o)")))
                        vec.wait_ge(g_loaded, h() * 16)
                        need(vec, ob_turned, h(-2))
                        own.done(tt(decay, g_row, hcol[:, TAB_G].unsqueeze(3).to_broadcast([P, 2, NT, P]), ALU.subtract))
                        tt(decay, decay, far.unsqueeze(2).to_broadcast([P, 2, NT, P]), ALU.add).then_inc(decay_arg, 1)
                        vec.wait_ge(decay_arg, h())

                    def qk_sums():
                        vec.wait_ge(qk_squared, h())
                        V.tensor_reduce(small[:, c0:8], sq_b[:, c0:], AX, ALU.add).then_inc(qk_summed, 1)
                        vec.wait_ge(qk_summed, h())

                    def qk_norm():
                        vec.wait_ge(qk_rms, h())
                        flat = ps[:, G0:G0 + 2, :].rearrange("p b (c d) -> p (b c) d", d=P)
                        tt(qk_tok[:, c0:], flat[:, c0:], small[:, 8 + c0:16].unsqueeze(2).to_broadcast([P, 8 - c0, P]),
                           ALU.mult).then_inc(qk_normed, 1)
                        vec.wait_ge(qk_normed, h())

                    def gram_terms():
                        vec.wait_ge(grams, h())
                        vec.wait_ge(decay_ready, h())
                        for d in range(2):
                            own.go(V.scalar_tensor_tensor(att_T[:, d, c0:], quads(G3)[:, c0:], float(P) ** -0.5, decay[:, d, c0:],
                                                          ALU.mult, ALU.mult))
                            for cc in range(NT):
                                own.go(V.scalar_tensor_tensor(m_T[:, d, cc], quads(G2)[:, cc], hcol[:, TAB_BETA, d, cc:cc + 1],
                                                              decay[:, d, cc], ALU.mult, ALU.mult))
                        own.settle()

                    def start_inverse(d):
                        mk = msk[:, 0, 1 - d].unsqueeze(1).to_broadcast([P, NT, P])
                        own.done(V.scalar_tensor_tensor(inv_T[:, d], m_T[:, d], -1.0, mk, ALU.mult, ALU.mult))
                        tt(inv_T[:, d], inv_T[:, d], ident.unsqueeze(1).to_broadcast([P, NT, P]), ALU.add).then_inc(inv_started, 1)
                        vec.wait_ge(inv_started, h(-1, 2, d + 1))

                    def q_decay():
                        vec.wait_ge(qk_T_ready, h())
                        for d in range(2):
                            m = V.scalar_tensor_tensor(q_dec[:, d, c0:], qk_T[:, c0:NT], float(P) ** -0.5, q_dec[:, d, c0:],
                                                       ALU.mult, ALU.mult)
                            if d == 0:
                                own.go(m)
                        m.then_inc(q_decayed, 1)
                        own.settle()
                        vec.wait_ge(q_decayed, h())

                    def mask_x(d, n):
                        vec.wait_ge(x_product[d], h(-1, LVL, n + 1))
                        tt(prod[:, d], quads(GX[d]), msk[:, n + 1, d].unsqueeze(1).to_broadcast([P, NT, P]),
                           ALU.mult).then_inc(x_masked[d], 1)
                        vec.wait_ge(x_masked[d], h(-1, LVL, n + 1))

                    def merge(d, n):
                        vec.wait_ge(t_product[d], h(-1, LVL, n + 1))
                        if n < LVL - 1:
                            own.go(tt(inv[:, d], inv[:, d], quads(GX[d]), ALU.subtract))
                        tt(inv_T[:, d], inv_T[:, d], quads(GT[d]), ALU.subtract).then_inc(t_merged[d], 1)
                        vec.wait_ge(t_merged[d], h(-1, LVL, n + 1))
                        own.settle()

                    def state(j):
                        vec.wait_ge(s_product, h(-1, 3, j + 1))
                        for d in range(2):
                            ch = ORDER[d][j]
                            dst = states[:, d, j + 1]
                            if j == 0:
                                m = V.tensor_copy(dst, ps[:, GT[d], 0:P])
                            else:
                                m = V.scalar_tensor_tensor(dst, states[:, d, j], hcol[:, TAB_LAST, d, ch:ch + 1],
                                                           ps[:, GT[d], 0:P], ALU.mult, ALU.add)
                            if d == 0:
                                own.go(m)
                        m.then_inc(s_ready, 1)
                        own.settle()
                        vec.wait_ge(s_ready, h(-1, 3, j + 1))

                    def ob_sums():
                        vec.wait_ge(ob_squared, h())
                        V.tensor_reduce(small[:, 16 + c0:20], sq_b[:, c0:NT], AX, ALU.add).then_inc(ob_summed, 1)
                        vec.wait_ge(ob_summed, h())

                    def ob_norm():
                        vec.wait_ge(ob_rms, h())
                        tt(o_b[:, c0:], quads(G0)[:, c0:], small[:, 20 + c0:24].unsqueeze(2).to_broadcast([P, NT - c0, P]),
                           ALU.mult).then_inc(ob_normed, 1)
                        vec.wait_ge(ob_normed, h())

                    def y_out(which):
                        turned, src, z, yy, ready, stored = (
                            (oa_turned, A0, z_a, y_a, ya_ready, ya_stored), (ob_turned, G1, z_b, y_b, yb_ready, yb_stored))[which]
                        vec.wait_ge(turned, h())
                        need(vec, stored, h(-2) * 16)
                        V.scalar_tensor_tensor(yy[:, c0 * P:], ps[:, src, c0 * P:], halfw[:, layer, which:which + 1],
                                               z[:, c0 * P:], ALU.mult, ALU.mult).then_inc(ready, 1)
                        vec.wait_ge(ready, h())

                    def a_max(n):
                        qt = q_tiles[layer][n]
                        keys = T if qt >= 2 else N_CTX
                        vec.wait_ge(scored, nth_q(layer, i, -1, n + 1))
                        own.done(V.tensor_reduce(small[:, 32:34], ps[:, A0:A0 + 2, 0:keys], AX, ALU.max))
                        V.tensor_scalar(small[:, 34:36], small[:, 32:34], -0.125, None, ALU.mult).then_inc(maxed, 1)
                        vec.wait_ge(maxed, nth_q(layer, i, -1, n + 1))

                    def a_mix(n):
                        qt = q_tiles[layer][n]
                        keys = T if qt >= 2 else N_CTX
                        vec.wait_ge(exped, nth_q(layer, i, -1, n + 1))
                        own.done(V.reciprocal(small[:, 38:40], small[:, 36:38]))
                        own.done(V.tensor_scalar(prob[:, 1, 0:keys], prob[:, 1, 0:keys], small[:, 39:40], lam[:, layer:layer + 1],
                                                 ALU.mult, ALU.mult))
                        V.scalar_tensor_tensor(prob[:, 0, 0:keys], prob[:, 0, 0:keys], small[:, 38:39], prob[:, 1, 0:keys],
                                               ALU.mult, ALU.add).then_inc(mixed, 1)
                        vec.wait_ge(mixed, nth_q(layer, i, -1, n + 1))

                    def oa_sums():
                        vec.wait_ge(oa_squared, h())
                        V.tensor_reduce(small[:, 24 + c0:28], sq_a[:, 0, c0 * P:].rearrange("p (c d) -> p c d", d=P), AX,
                                        ALU.add).then_inc(oa_summed, 1)
                        vec.wait_ge(oa_summed, h())

                    def oa_norm():
                        vec.wait_ge(oa_rms, h())
                        tt(o_a[:, c0:], o_a[:, c0:], small[:, 28 + c0:32].unsqueeze(2).to_broadcast([P, NT - c0, P]),
                           ALU.mult).then_inc(oa_normed, 1)
                        vec.wait_ge(oa_normed, h())

                    def ada(k):
                        lay, firstb = ada_block(layer, k)
                        mod_column(i * ADA_IN[layer] + (ada_before(layer) + k + 1), lay, i * 2 + (firstb + k % 2))

                    plan = {}

                    def put(s, f, *a):
                        plan.setdefault(s, []).append((f, a))

                    nq = len(q_tiles[layer])
                    if fill:
                        put(0, decay_args)
                        put(1, z_silu, -1, 1)
                        put(2, qk_sums)
                        for n in range(nq):
                            put(3 + 8 * n, a_max, n)
                            put(6 + 8 * n, a_mix, n)
                        put(5, qk_norm)
                        put(9, gram_terms)
                        put(11, start_inverse, 0)
                        put(12, start_inverse, 1)
                        put(13, q_decay)
                        for n in range(LVL):
                            put(15 + 4 * n, mask_x, 0, n)
                            put(16 + 4 * n, mask_x, 1, n)
                            put(17 + 4 * n, merge, 0, n)
                            put(18 + 4 * n, merge, 1, n)
                        for j in range(3):
                            put(44 + 4 * j, state, j)
                        put(57, ob_sums)
                        put(60, ob_norm)
                        put(62, y_out, 1)
                        put(3 + 8 * nq, oa_sums)
                        put(5 + 8 * nq, oa_norm)
                        put(39, y_out, 0)
                    if project:
                        for x_ in range(3):
                            for j in range(CONV_K):
                                put(8 * x_ + 9 + j, tap, x_, j)
                            put(8 * x_ + 15, silu, x_)
                        put(41, rope, 0)
                        put(61, rope, 1)
                        put(58, z_silu, 0, 0)
                        for k in range(ADA_IN[layer]):
                            put(45 + 3 * k, ada, k)
                        if isinstance(i, int) and i == 0:
                            put(2, table_step, 0)
                            put(4, table_step, 1)
                            put(6, table_step, 2)
                    for s in range(SLOTS):
                        if project and s % 4 == 0:
                            split_lo(i, base + 2 + s // 4 + 1)
                        for f, a in plan.get(s, ()):
                            f(*a)
                    own.finish()

                split_lo(0, base + 2)
                own.finish()
                heads(vec, layer, body)

                own.finish()
                first = base + 2 + HEADS * UNITS
                for k in range(KT):
                    vec.wait_ge(y_hi_ready, layer * KT + k + 1)
                    tt(h_lo[:, k, c0 * P:], y_in[:, k % 2, c0 * P:], h_hi[:, k, c0 * P:].bitcast(F32),
                       ALU.subtract).then_inc(y_split, 1)
                    vec.wait_ge(y_split, layer * KT + k + 1)
                own.done(V.memset(sq_sum, 0.0))
                for n in range(KT):
                    for half in range(2):
                        u = first + 2 * n + half + 1
                        if half == 0 or n < KT - 1:
                            split_lo(0, u)
                    vec.wait_ge(w_used, first + 2 * n + 2)
                    vec.wait_ge(old_loaded[n % 2], 16 * (layer * HEADS + n // 2 + 1))
                    for v in range(c0 // 2, 2):
                        seg = slice(v * N_CTX, (v + 1) * N_CTX)
                        m = V.scalar_tensor_tensor(xT[:, n, seg], ps[:, PJ + n % 2, seg], mod[:, layer, 2 * KT + n, v:v + 1],
                                                   x_old[:, n % 2, seg], ALU.mult, ALU.add)
                        if v == 0:
                            own.go(m)
                    m.then_inc(out_added, 1)
                    own.settle() if c0 == 0 else None
                    vec.wait_ge(out_added, layer * KT + n + 1)
                    vec.wait_ge(x_squared, (layer + 1) * KT + n + 1)
                    tt(sq_sum[:, c0 * P:], sq_sum[:, c0 * P:], sq_tile[:, c0 * P:], ALU.add).then_inc(sums_ready, 1)
                    vec.wait_ge(sums_ready, layer * KT + n + 1)

            rms(DEPTH, N_CTX // P)
            vec.wait_ge(rms_copied, DEPTH + 1)
            for k in range(KT):
                V.scalar_tensor_tensor(xT[:, k, N_CTX:], xT[:, k, N_CTX:], vecs[:, 0, 64 + k:65 + k], x_rms[:, N_CTX:],
                                       ALU.mult, ALU.mult).then_inc(fin_scaled, 1)

        @block.gpsimd
        def _(pool):
            own = Count(pool, pool_step)
            G = nc.gpsimd
            pool.dma_start(msk[:].rearrange("p n x d -> p (n x d)"), masks).then_inc(masks_loaded, 16)
            pool.wait_ge(staged, 1)

            def power(dst, src, n, scale, eps, signal, value):
                own.note()
                own.done(G.tensor_scalar(dst, src, scale, eps, ALU.mult, ALU.add))
                G.tensor_tensor(dst, dst, minus_half[:, 0:n], ALU.pow).then_inc(signal, 1)
                pool.wait_ge(signal, value)

            def rms(n, c0):
                pool.wait_ge(sums_copied, n + 1)
                power(small[:, 44 + c0:48], small[:, 44 + c0:48], NT - c0, 1.0 / D, NORM_EPS, rms_ready, n + 1)

            for layer in range(DEPTH):
                c0 = first_q(layer)
                own.finish()
                rms(layer, 0)

                def body(i, project, fill):
                    own.finish()
                    if not fill:
                        return

                    def h(off=-1, per=1, idx=1):
                        return nth(layer, i, off, per, idx)

                    pool.wait_ge(qk_summed, h())
                    power(small[:, 8 + c0:16], small[:, c0:8], 8 - c0, 1.0, 4e-6, qk_rms, h())
                    pool.wait_ge(qk_normed, h())
                    need(pool, w_product, h(-2, 2, 2))
                    need(pool, s_product, h(-2, 3, 3))
                    for d in range(2):
                        for n, dst in ((TAB_GROW, k_grow), (TAB_END, k_end)):
                            m = G.tensor_tensor(dst[:, d], qk_tok[:, NT:], hcol[:, n, d].unsqueeze(2).to_broadcast([P, NT, P]),
                                                ALU.mult)
                            if (d, n) != (1, TAB_END):
                                own.go(m)
                    m.then_inc(k_scaled, 1)
                    own.settle()
                    pool.wait_ge(k_scaled, h())
                    pool.wait_ge(oa_summed, h())
                    power(small[:, 28 + c0:32], small[:, 24 + c0:28], NT - c0, 1.0 / P, SUBLN_EPS, oa_rms, h())
                    pool.wait_ge(ob_summed, h())
                    power(small[:, 20 + c0:24], small[:, 16 + c0:20], NT - c0, 1.0 / P, NORM_EPS, ob_rms, h())
                    own.finish()

                own.finish()
                heads(pool, layer, body)

                pool.wait_ge(ya_stored, 16 * HEADS * (layer + 1))
                pool.wait_ge(yb_stored, 16 * HEADS * (layer + 1))
                pool.wait_ge(yb_ready, HEADS * (layer + 1))
                for k in range(KT):
                    if k >= 2:
                        pool.wait_ge(y_split, layer * KT + k - 1)
                    pool.dma_start(y_in[:, k % 2, c0 * P:], y_dram[layer, k, :, c0 * P:]).then_inc(y_loaded[k % 2], 16)
                pool.wait_ge(x_stored, 16 * (1 + layer * KT))
                for n in range(KT):
                    if n >= 2:
                        pool.wait_ge(out_added, layer * KT + n - 1)
                    pool.dma_start(x_old[:, n % 2, c0 * P:], x_dram[n, :, c0 * P:]).then_inc(old_loaded[n % 2], 16)
            own.finish()
            rms(DEPTH, N_CTX // P)

        @block.tensor
        def _(pe):
            mm = nc.tensor.matmul
            turn = nc.tensor.transpose

            pe.wait_ge(consts_loaded, 16)
            pe.wait_ge(rows_loaded, 16 * 12)
            for b in range(4):
                last = turn(ps[:, A0, b * P:(b + 1) * P], rows_in[:, b], ident)
            last.then_inc(setup_turned, 1)

            def turn_x(n):
                pe.wait_ge(x_loaded[n % 2], 16 * (n // 2 + 1))
                for q in range(4):
                    if n >= 1:
                        pe.wait_ge(x_evacuated, (n - 1) * 4 + q + 1)
                    for k in range(4 * q, 4 * q + 4):
                        last = turn(ps[:, G0 + q, (k % 4) * P:(k % 4 + 1) * P], x_in[:, n % 2, k * P:(k + 1) * P], ident)
                    last.then_inc(x_turned, 1)

            def ada_multiply(slots, loads, prior):
                need(pe, ada_copied, prior)
                for half in range(2):
                    pe.wait_ge(slots[half][1], loads[half])
                    for k in range(HALF):
                        kt = half * HALF + k
                        j = kt % 4
                        last = mm(ps[32 * j:32 * j + 32, A0, 0:P], c_T[:, kt, :], slots[half][0][:, k, :],
                                  start=kt < 4, stop=kt >= KT - 4)
                        if k == HALF - 1:
                            last.then_inc(ada_used, 1)

            def ada_turn(value):
                pe.wait_ge(ada_copied, value)
                need(pe, mod_ready, value - 1)
                mm(bank(A1, 2), ada_sb[:], sel, start=True, stop=True).then_inc(ada_turned, 1)

            pe.wait_ge(staged, 2)
            for b in range(ADA_START):
                if b % 4 == 1 and b // 4 < NT:
                    turn_x(b // 4)
                sl = [(ada_ring[(2 * b + hf) % 6], ada_loaded[(2 * b + hf) % 6]) for hf in range(2)]
                ada_multiply(sl, [16 * ((2 * b + hf) // 6 + 1) for hf in range(2)], b)
                ada_turn(b + 1)

            def rms(n, ready, value, c0):
                pe.wait_ge(ready, value)
                for cc in range(c0, NT):
                    last = mm(ps[:, A0, cc:cc + 1], sq_sum[:, cc * P:(cc + 1) * P], ones[:, 0:1], start=True, stop=True)
                last.then_inc(sums_turned, 1)
                pe.wait_ge(diag_ready, n + 1)
                mm(ps[:, A1, c0 * P:], ones, diag[:, c0 * P:], start=True, stop=True).then_inc(rms_spread, 1)

            for layer in range(DEPTH):
                base = layer * LAYER_UNITS
                c0 = first_q(layer)
                if layer == 0:
                    rms(0, vec_setup, KT, 0)
                else:
                    rms(1, sums_ready, KT, 0)

                def unit_piece(u, bank_, t0, half, ks, signal=None):
                    s = u % 2
                    for k in ks:
                        kt = half * HALF + k
                        o = ps[:, bank_, t0:]
                        mm(o, w_hi[:, s, k], h_hi[:, kt, t0:], start=kt == 0, stop=False)
                        mm(o, w_hi[:, s, k], h_lo[:, kt, t0:], start=False, stop=False)
                        last = mm(o, w_lo[:, s, k], h_hi[:, kt, t0:], start=False, stop=kt == KT - 1)
                    return last

                if layer == 1:
                    pe.wait_ge(evacuated, LAYER_TILES)
                for half in range(2):
                    pe.wait_ge(w_split, base + half + 1)
                    for k in range(HALF):
                        pe.wait_ge(h_ready, layer * KT + half * HALF + k + 1)
                        last = unit_piece(base + half, PJ, 0, half, [k])
                    last.then_inc(w_used, 1)

                def table_step(s):
                    if s == 0:
                        pe.wait_ge(evacuated, layer * LAYER_TILES + 1)
                        for cc in range(NT):
                            last = turn(ps[:, A0, cc * 32:(cc + 1) * 32], th[96:128, cc * P:(cc + 1) * P], ident[96:128, 96:128])
                        last.then_inc(ab_turned, 1)
                    if s == 1:
                        pe.wait_ge(tab_beta, layer + 1)
                        gx = decay[:, 0, 0, 0:NT * 16].rearrange("p (c n) -> p c n", c=NT)
                        for n in range(4):
                            d = n % 2
                            lhs = cst[:, C_TRI + d * P:C_TRI + (d + 1) * P] if n < 2 else ones
                            last = mm(ps[:, A1, n * 32:(n + 1) * 32], lhs, gx[:, :, 8 * d:8 * d + 8], start=True, stop=True)
                        last.then_inc(tab_sums, 1)
                    if s == 2:
                        pe.wait_ge(tab_ready, layer + 1)
                        for cc in range(NT):
                            last = turn(ps[0:16, A0, cc * P:(cc + 1) * P], decay[:, 0, 1, 16 * cc:16 * cc + 16], ident)
                        last.then_inc(tab_rows, 1)

                def body(i, project, fill):
                    def h(off=-1, per=1, idx=1):
                        return nth(layer, i, off, per, idx)

                    def turn_qk():
                        pe.wait_ge(qkv_ready, h(-1, 3, 3))
                        need(pe, yb_ready, h(-2))
                        for n in range(c0, 8):
                            x_, cc = n // NT, n % NT
                            last = turn(ps[:, G0 + x_, cc * P:(cc + 1) * P], qkv[:, x_, cc * P:(cc + 1) * P], ident)
                        last.then_inc(qk_turned, 1)

                    def turn_v():
                        for cc in range(NT):
                            last = turn(ps[:, G2, cc * P:(cc + 1) * P], qkv[:, 2, cc * P:(cc + 1) * P], ident)
                        last.then_inc(v_turned, 1)

                    def turn_back():
                        pe.wait_ge(qk_normed, h())
                        for n in range(c0, 8):
                            last = turn(ps[:, G0 + n // NT, (n % NT) * P:(n % NT + 1) * P], qk_tok[:, n], ident)
                        last.then_inc(qk_returned, 1)

                    def gram():
                        pe.wait_ge(qk_T_ready, h())
                        pe.wait_ge(vb_ready, h())
                        for cc in range(NT):
                            last = mm(quads(G2)[:, cc], qk_T[:, NT + cc], qk_T[:, NT + cc], start=True, stop=True)
                        for cc in range(c0, NT):
                            last = mm(quads(G3)[:, cc], qk_T[:, NT + cc], qk_T[:, cc], start=True, stop=True)
                        last.then_inc(grams, 1)

                    def turn_inv(d):
                        pe.wait_ge(inv_started, h(-1, 2, d + 1))
                        for cc in range(NT):
                            last = turn(quads(GT[d])[:, cc], inv_T[:, d, cc], ident)
                        last.then_inc(inv_turned, 1)

                    def times_m(d, n):
                        if n == 0:
                            pe.wait_ge(inv_copied, h(-1, 2, d + 1))
                        else:
                            pe.wait_ge(t_merged[d], h(-1, LVL, n))
                        for cc in range(NT):
                            last = mm(quads(GX[d])[:, cc], m_T[:, d, cc], inv[:, d, cc], start=True, stop=True)
                        last.then_inc(x_product[d], 1)

                    def times_inv(d, n):
                        pe.wait_ge(x_masked[d], h(-1, LVL, n + 1))
                        for cc in range(NT):
                            if n < LVL - 1:
                                mm(quads(GX[d])[:, cc], inv_T[:, d, cc], prod[:, d, cc], start=True, stop=True)
                            last = mm(quads(GT[d])[:, cc], prod[:, d, cc], inv_T[:, d, cc], start=True, stop=True)
                        last.then_inc(t_product[d], 1)

                    def w_mul(d):
                        pe.wait_ge(t_merged[d], h(-1, LVL, LVL))
                        pe.wait_ge(k_scaled, h())
                        for cc in range(NT):
                            last = mm(quads(GX[d])[:, cc], k_grow[:, d, cc], inv_T[:, d, cc], start=True, stop=True)
                        last.then_inc(w_product, 1)

                    def v_mul(j):
                        if j == 0:
                            pe.wait_ge(w_ready, h(-1, 2, 2))
                        else:
                            pe.wait_ge(s_ready, h(-1, 3, j))
                        for d in range(2):
                            ch = ORDER[d][j]
                            last = mm(ps[:, GT[d], 0:P], inv_T[:, d, ch], v_tok[:, ch], start=True, stop=j == 0)
                            if j:
                                last = mm(ps[:, GT[d], 0:P], w_T[:, d, ch], states[:, d, j], start=False, stop=True)
                        last.then_inc(v_product, 1)

                    def s_mul(j):
                        pe.wait_ge(v_ready, h(-1, 4, j + 1))
                        for d in range(2):
                            ch = ORDER[d][j]
                            last = mm(ps[:, GT[d], 0:P], k_end[:, d, ch], v_new[:, d, ch], start=True, stop=True)
                        last.then_inc(s_product, 1)

                    def o_mul():
                        pe.wait_ge(v_ready, h(-1, 4, 4))
                        pe.wait_ge(q_decayed, h())
                        for cc in range(c0, NT):
                            terms = []
                            for d in range(2):
                                terms.append((att_T[:, d, cc], v_new[:, d, cc]))
                                j = ORDER[d].index(cc)
                                if j:
                                    terms.append((q_dec[:, d, cc], states[:, d, j]))
                            for n, (a, b) in enumerate(terms):
                                last = mm(quads(G0)[:, cc], a, b, start=n == 0, stop=n == len(terms) - 1)
                        last.then_inc(ob_product, 1)

                    def turn_ob():
                        pe.wait_ge(ob_normed, h())
                        for cc in range(c0, NT):
                            last = turn(quads(G1)[:, cc], o_b[:, cc], ident)
                        last.then_inc(ob_turned, 1)

                    def turn_va():
                        need(pe, rope_done, h(-1, 2, 2))
                        for cc in range(NT):
                            last = turn(quads(A0)[:, cc], a_v[:, cc * P:(cc + 1) * P], ident)
                        last.then_inc(va_turned, 1)

                    def score(n):
                        qt = q_tiles[layer][n]
                        keys = T if qt >= 2 else N_CTX
                        if n == 0:
                            pe.wait_ge(va_ready, h())
                            pe.wait_ge(mod_ready, ada_before(layer) + i * ADA_IN[layer])
                        else:
                            pe.wait_ge(oa_copied, nth_q(layer, i, -1, n))
                        for m in range(2):
                            r = slice(64 * m, 64 * m + 64)
                            last = mm(bank(A0 + m, keys), a_q[r, qt * P:(qt + 1) * P], a_k[r, 0:keys], start=True, stop=True)
                        last.then_inc(scored, 1)

                    def turn_p(n):
                        kt = NT if q_tiles[layer][n] >= 2 else 2
                        pe.wait_ge(mixed, nth_q(layer, i, -1, n + 1))
                        for cc in range(kt):
                            last = turn(quads(A0)[:, cc], prob[:, 0, cc * P:(cc + 1) * P], ident)
                        last.then_inc(p_turned, 1)

                    def attend(n):
                        kt = NT if q_tiles[layer][n] >= 2 else 2
                        pe.wait_ge(p_copied, nth_q(layer, i, -1, n + 1))
                        for cc in range(kt):
                            last = mm(bank(A1, P), prob_T[:, cc], va_tok[:, cc], start=cc == 0, stop=cc == kt - 1)
                        last.then_inc(oa_product, 1)

                    def turn_oa():
                        pe.wait_ge(oa_normed, h())
                        for cc in range(c0, NT):
                            last = turn(quads(A0)[:, cc], o_a[:, cc], ident)
                        last.then_inc(oa_turned, 1)

                    def rotate(n):
                        t = (AK, AQ)[n]
                        pe.wait_ge(evacuated, i * TILES + (layer * LAYER_TILES + 1 + t + 1))
                        if isinstance(i, int) and i == 0:
                            pe.wait_ge(rows_copied, layer + 1)
                        elif n == 0:
                            pe.wait_ge(ya_ready, h())
                        mm(bank(A0, N_CTX), rot, a_raw, start=True, stop=True).then_inc(rot_done, 1)

                    def ada(k):
                        if k == 0:
                            pe.wait_ge(rope_done, nth(layer, i, 0, 2, 1))
                        first_loads = ada_before(layer)
                        at_start = [len([u for u in range(2 * ADA_START) if u % 6 == 4 + hf]) for hf in range(2)]
                        n = first_loads - ADA_START + k
                        loads = [i * (16 * ADA_IN[layer]) + 16 * (at_start[hf] + n + 1) for hf in range(2)]
                        sl = [(ada_raw[:, hf], ada_loaded[4 + hf]) for hf in range(2)]
                        v = i * ADA_IN[layer] + (first_loads + k)
                        ada_multiply(sl, loads, v)

                    def ada_t(k):
                        ada_turn(i * ADA_IN[layer] + (ada_before(layer) + k + 1))

                    plan = {}

                    def put(s, f, *a):
                        plan.setdefault(s, []).append((f, a))

                    nq = len(q_tiles[layer])
                    if fill:
                        put(0, turn_qk)
                        put(1, turn_v)
                        put(0, turn_va)
                        put(5, turn_back)
                        put(8, gram)
                        put(13, turn_inv, 0)
                        put(14, turn_inv, 1)
                        for n in range(LVL):
                            put(15 + 4 * n, times_m, 0, n)
                            put(16 + 4 * n, times_m, 1, n)
                            put(17 + 4 * n, times_inv, 0, n)
                            put(18 + 4 * n, times_inv, 1, n)
                        put(39, w_mul, 0)
                        put(40, w_mul, 1)
                        for j in range(4):
                            put(42 + 4 * j, v_mul, j)
                            if j < 3:
                                put(44 + 4 * j, s_mul, j)
                        put(56, o_mul)
                        put(61, turn_ob)
                        for n in range(nq):
                            put(2 + 8 * n, score, n)
                            put(7 + 8 * n, turn_p, n)
                            put(9 + 8 * n, attend, n)
                        put(6 + 8 * nq, turn_oa)
                    if project:
                        put(40, rotate, 0)
                        put(60, rotate, 1)
                        for k in range(ADA_IN[layer]):
                            put(42 + 3 * k, ada, k)
                            put(44 + 3 * k, ada_t, k)
                        if isinstance(i, int) and i == 0:
                            put(2, table_step, 0)
                            put(5, table_step, 1)
                            put(8, table_step, 2)
                    for s in range(SLOTS):
                        if project:
                            k = s // 4
                            t, half = k // 2, k % 2
                            if s % 4 == 0:
                                pe.wait_ge(w_split, i * UNITS + (base + 2 + k + 1))
                                if half == 0:
                                    pe.wait_ge(evacuated, i * TILES + (layer * LAYER_TILES + 1 + t - 1))
                            last = unit_piece(base + 2 + k, PJ + (1 + t) % 2, tokens(layer, t), half,
                                              [2 * (s % 4), 2 * (s % 4) + 1])
                            if s % 4 == 3:
                                last.then_inc(w_used, 1)
                        for f, a in plan.get(s, ()):
                            f(*a)

                heads(pe, layer, body)

                first = base + 2 + HEADS * UNITS
                for n in range(KT):
                    for half in range(2):
                        u = first + 2 * n + half
                        pe.wait_ge(w_split, u + 1)
                        if half == 0 and n >= 2:
                            pe.wait_ge(out_added, layer * KT + n - 1)
                        for k in range(HALF):
                            if n == 0:
                                pe.wait_ge(y_split, layer * KT + half * HALF + k + 1)
                            last = unit_piece(u, PJ + n % 2, c0 * P, half, [k])
                        last.then_inc(w_used, 1)

            rms(DEPTH, sums_ready, DEPTH * KT, N_CTX // P)
            for n in range(2):
                for q in range(4):
                    if n == 1:
                        pe.wait_ge(fin_copied, q + 1)
                    for k in range(4 * q, 4 * q + 4):
                        pe.wait_ge(fin_scaled, k + 1)
                        last = turn(ps[:, G0 + q, (k % 4) * P:(k % 4 + 1) * P],
                                    xT[:, k, (2 + n) * P:(3 + n) * P], ident)
                    last.then_inc(fin_turned, 1)


_INS = ['x', 'c', 'ctx', 'c_ctx', 'w_ada', 'b_ada', 'norm_w', 'w_in', 'conv_w', 'dn_a_log', 'dn_dt_bias',
        'dn_norm_w', 'diff_lambda', 'subln_w', 'w_out', 'final_norm_w']


def kernel(**inputs):
    import ml_dtypes
    import concourse.bacc as _bacc
    from concourse.bass_utils import run_bass_kernel_spmd as _run

    consts, masks = shape_constants()
    nc = _bacc.Bacc("TRN2", target_bir_lowering=False, num_devices=1)
    arrays, args = {}, []
    for name in _INS:
        arrays[f"in_{name}"] = np.ascontiguousarray(inputs[name])
    arrays["in_consts"] = consts
    arrays["in_masks"] = masks.astype(ml_dtypes.bfloat16)
    for name, a in arrays.items():
        args.append(nc.dram_tensor(name, a.shape, mybir.dt.from_np(a.dtype), kind="ExternalInput").ap())
    args.append(nc.dram_tensor("out", inputs["x"].shape, F32, kind="ExternalOutput").ap())
    build_trunk(nc, *args)
    r = _run(nc, [arrays], core_ids=[0])
    return r.results[0]["out"]
```

```python
from contextlib import ExitStack

import numpy as np

import concourse.bass as bass
from concourse import mybir

ALU = mybir.AluOpType
ACT = mybir.ActivationFunctionType
AX = mybir.AxisListType.X
F32 = mybir.dt.float32
F32R = mybir.dt.float32r
BF16 = mybir.dt.bfloat16

P = 128
D = 2048
KT = D // P
N_CTX = 256
T = 512
NT = T // P
DEPTH = 2
HEADS = 8
GRID_W = 64
QK_A = V_A = QK_B = V_B = 1024
CONV_K = 5
N_IN = 2 * QK_A + 2 * V_A + 2 * QK_B + V_B + V_B + 4 * HEADS
HALF = KT // 2
UNIT = HALF * P
TILES = 8
UNITS = 2 * TILES
SLOTS = 4 * UNITS
PAD = CONV_K // 2
SEG = N_CTX + 2 * PAD
NORM_EPS = 1e-6
SUBLN_EPS = 1e-5
FAR = -1.0e30
LEVELS = (16, 32, 64)
BLK = LEVELS[0]
NB = P // BLK
OUT_HEADS = HEADS - 1
OUT_UNITS = 2 * KT
LAST_UNITS = KT // 4

BQ, BK, BV, AK, AV, AQ, ZA, ZB = range(TILES)
BASE_B = 2 * QK_A + 2 * V_A
COLUMN = {BQ: BASE_B, BK: BASE_B + QK_B, BV: BASE_B + 2 * QK_B, AK: QK_A, AV: 2 * QK_A,
          AQ: 0, ZA: 2 * QK_A + V_A, ZB: BASE_B + 2 * QK_B + V_B}

C_ID = 0
C_TRI = C_ID + P
C_FAR = C_TRI + 2 * P
C_ONE = C_FAR + 2 * P
C_ROT = C_ONE + P
C_COS = C_ROT + P
C_SIN = C_COS + N_CTX
C_SEL = C_SIN + N_CTX
C_END = C_SEL + 2


def shape_constants():
    i = np.arange(P)
    c = np.zeros((P, C_END), np.float32)
    c[:, C_ID:C_ID + P] = np.eye(P)
    before = (i[:, None] <= i[None, :]).astype(np.float32)
    c[:, C_TRI:C_TRI + P] = before
    c[:, C_TRI + P:C_TRI + 2 * P] = before.T
    c[:, C_FAR:C_FAR + P] = (1 - before) * FAR
    c[:, C_FAR + P:C_FAR + 2 * P] = (1 - before.T) * FAR
    c[:, C_ONE:C_ONE + P] = 1.0
    half = 32
    for m in range(P):
        d = m % (2 * half)
        c[m + half if d < half else m - half, C_ROT + m] = -1.0 if d < half else 1.0
    freqs = half // 2
    inv = np.float32(10000.0) ** (-np.arange(freqs, dtype=np.float32) / np.float32(freqs))
    tok = np.arange(N_CTX)
    rows = (tok // GRID_W).astype(np.float32)
    cols = (tok % GRID_W).astype(np.float32)
    ang = np.concatenate([rows[:, None] * inv, cols[:, None] * inv], axis=-1).astype(np.float32)
    c[:, C_COS:C_COS + N_CTX] = np.cos(ang).T[i % half]
    c[:, C_SIN:C_SIN + N_CTX] = np.sin(ang).T[i % half]
    for v in range(2):
        c[:, C_SEL + v] = i % 32 == v
    m = np.zeros((P, len(LEVELS), 2, P), np.float32)
    for n, b in enumerate(LEVELS):
        blk = i // b
        low = (blk[None, :] % 2 == 0) & (blk[:, None] == blk[None, :] + 1)
        m[:, n, 0] = low
        m[:, n, 1] = low.T
    return c, m.reshape(P, -1)


class Count:

    def __init__(self, eng, sem):
        self.eng, self.sem, self.n = eng, sem, 0

    def finish(self):
        if self.n:
            self.note()
            self.settle()
            self.eng.sem_clear(self.sem)
            self.n = 0

    def done(self, ins):
        self.go(ins)
        self.eng.wait_ge(self.sem, self.n)

    def go(self, ins):
        ins.then_inc(self.sem, 1)
        self.n += 1

    def note(self):
        self.eng.sem_inc(self.sem, 1)
        self.n += 1

    def settle(self):
        self.eng.wait_ge(self.sem, self.n)


def need(eng, sem, value):
    if not isinstance(value, int) or value > 0:
        eng.wait_ge(sem, value)


def build_trunk(nc, x, c, ctx_in, c_ctx, w_ada, b_ada, norm_w, w_in, conv_w, dn_a_log, dn_dt_bias,
                dn_norm_w, diff_lambda, subln_w, w_out, final_norm_w, consts, masks, out):
    x_dram = nc.dram_tensor("x_channel_major", [KT, P, T], F32).ap()
    y_dram = nc.dram_tensor("mixed", [DEPTH, KT, P, T], F32).ap()
    g_dram = nc.dram_tensor("decay_rows", [DEPTH, 2 * HEADS, T], F32).ap()
    m_dram, s_dram = [nc.dram_tensor(n, [2 * NT * (P * P + P)], F32).ap() for n in ("m_chunks", "s_chunks")]

    def chunk_rows(t):
        return t.rearrange("(x q) -> x q", x=2 * NT)[:, 0:P * P].rearrange("x (p n) -> p x n", n=P)

    def diagonal_blocks(t):
        return t.rearrange("(p q) -> p q", p=2 * NT * NB)[:, 0:BLK * P].rearrange("p (r n) -> p r n", n=P)[:, :, 0:BLK]

    toks = [ctx_in.rearrange("b n d -> (b n) d"), x.rearrange("b n d -> (b n) d")]
    out2 = out.rearrange("b n d -> (b n) d")
    lam_init = [0.8 - 0.6 * float(np.exp(-0.3 * i)) for i in range(DEPTH)]

    with ExitStack() as ctx:
        def sb(name, shape, dt=F32):
            return ctx.enter_context(nc.sbuf_tensor(name, shape, dt))

        def sem(name):
            return ctx.enter_context(nc.semaphore(name))

        h_hi = sb("h_hi", [P, KT, T], F32R)
        h_lo = sb("h_lo", [P, KT, T], F32R)
        w_raw = sb("w_raw", [P, 4, HALF, P])
        w_hi = sb("w_hi", [P, 2, HALF, P], F32R)
        w_lo = sb("w_lo", [P, 2, HALF, P], F32R)
        ada_raw = sb("ada_raw", [P, 2, HALF, P])
        ada_sb = sb("ada_sb", [P, P])
        cst = sb("cst", [P, C_END])
        msk = sb("msk", [P, len(LEVELS), 2, P], BF16)
        vecs = sb("vecs", [P, 4, P])
        c_T = sb("c_T", [P, KT, 32])
        mod = sb("mod", [P, DEPTH, 3 * KT, 2])
        scale_w = sb("scale_w", [P, KT, 2])
        tab = sb("tab", [P, 5, 2, NT, HEADS])
        hcol = sb("hcol", [P, 5, 2, NT])
        convh = sb("convh", [P, CONV_K, 3])
        lam = sb("lam", [P, DEPTH])
        alog = sb("alog", [P, 2, DEPTH, 2 * HEADS])
        small = sb("small", [P, 64])
        minus_half = sb("minus_half", [P, 8])
        halfw = sb("halfw", [P, DEPTH, 2])

        arena_size = 22300
        arena = sb("arena", [P, arena_size])
        at = [0]

        def carve(n):
            at[0] += n
            assert at[0] <= arena_size, at[0]
            return arena[:, at[0] - n:at[0]]

        cin = carve(2 * SEG).rearrange("p (s n) -> p s n", s=2)
        qkv = carve(3 * T).rearrange("p (x t) -> p x t", x=3)
        th = carve(T)
        a_q, a_k, a_v = carve(T), carve(T), carve(T)
        a_raw = carve(N_CTX)
        z_a, z_b = carve(T), carve(T)
        th_z = carve(T)
        qk_tok = carve(2 * T).rearrange("p (c d) -> p c d", d=P)
        qk_T = carve(2 * T).rearrange("p (c d) -> p c d", d=P)
        v_tok = carve(T).rearrange("p (c d) -> p c d", d=P)
        k_grow = carve(2 * T).rearrange("p (x c d) -> p x c d", x=2, d=P)
        k_end = carve(2 * T).rearrange("p (x c d) -> p x c d", x=2, d=P)
        q_dec = carve(2 * T).rearrange("p (x c d) -> p x c d", x=2, d=P)
        att_T = carve(2 * T).rearrange("p (x c d) -> p x c d", x=2, d=P)
        m_T = carve(2 * T).rearrange("p (x c d) -> p x c d", x=2, d=P)
        inv = carve(2 * T).rearrange("p (x c d) -> p x c d", x=2, d=P)
        inv_T = carve(2 * T).rearrange("p (x c d) -> p x c d", x=2, d=P)
        prod = carve(2 * T).rearrange("p (x c d) -> p x c d", x=2, d=P)
        g_row = carve(2 * T).rearrange("p (x c d) -> p x c d", x=2, d=P)
        decay = carve(2 * T).rearrange("p (x c d) -> p x c d", x=2, d=P)
        va_tok = carve(T).rearrange("p (c d) -> p c d", d=P)
        prob = carve(2 * T).rearrange("p (m n) -> p m n", m=2)
        prob_T = carve(T).rearrange("p (c d) -> p c d", d=P)
        o_a = carve(T).rearrange("p (c d) -> p c d", d=P)
        y_a, y_b = carve(T), carve(T)
        w_T = inv
        states = m_T
        v_new = prod
        o_b = decay[:, 0]
        sq_b = prod.rearrange("p x c d -> p (x c) d")
        sq_a = prob
        blocks = prod[0:2 * NT * NB].rearrange("p x c d -> p (x c d)")
        blk_m, blk_s, blk_t = [blocks[:, n * BLK * BLK:(n + 1) * BLK * BLK] for n in range(3)]
        x_part = (cin.rearrange("p s n -> p (s n)")[:, 0:T], th)
        at[0] = 0
        xT = carve(KT * T).rearrange("p (k t) -> p k t", k=KT)
        x_rms = carve(T)
        sq_tile = carve(T)
        sq_sum = carve(T)
        diag = carve(T)
        sq_tiles = (x_rms, sq_tile)
        x_squares = arena[:, at[0] - 4 * T:at[0]]
        h_tmp = carve(2 * T).rearrange("p (b t) -> p b t", b=2)
        ada_wide = carve(2 * T).rearrange("p (b t) -> p b t", b=2)
        at_xin = at[0]
        zeros = arena[:, arena_size - 2 * NT * P:]
        x_in = carve(2 * D).rearrange("p (b n) -> p b n", b=2)
        rows_in = carve(4 * P).rearrange("p (b n) -> p b n", b=4)
        lam_in = carve(DEPTH * 4 * 64)
        ada_ring = [w_raw[:, s] for s in range(4)] + [ada_raw[:, s] for s in range(2)]
        at[0] = at_xin
        o_row = carve(2 * D).rearrange("p (b n) -> p b n", b=2)

        ps = ctx.enter_context(nc.psum_tensor("ps", [P, 8, T], F32))
        PJ, G0, G1, G2, G3, A0, A1 = 0, 2, 3, 4, 5, 6, 7
        GX, GT = (G0, G2), (G1, G3)

        ident = cst[:, C_ID:C_ID + P]
        ones = cst[:, C_ONE:C_ONE + P]
        rot = cst[:, C_ROT:C_ROT + P]
        cos_t, sin_t = cst[:, C_COS:C_COS + N_CTX], cst[:, C_SIN:C_SIN + N_CTX]
        far = cst[:, C_FAR:C_FAR + 2 * P].rearrange("p (x d) -> p x d", x=2)
        sel = cst[:, C_SEL:C_SEL + 2]
        TAB_BETA, TAB_GROW, TAB_END, TAB_G, TAB_LAST = range(5)

        def sub(b):
            return b.rearrange("p (r n) -> p r n", r=BLK)

        def substitution(k, d):
            part = slice(d * NT * NB, (d + 1) * NT * NB)
            m, s_, t = [sub(b)[part] for b in (blk_m, blk_s, blk_t)]
            if d == 0:
                up = BLK - 1 - k
                return m[:, 0:up, up:up + 1], s_[:, up:up + 1, up:], s_[:, 0:up, up:], t[:, 0:up, up:]
            rows = slice(k + 1, BLK)
            return m[:, rows, k:k + 1], s_[:, k:k + 1, 0:k + 1], s_[:, rows, 0:k + 1], t[:, rows, 0:k + 1]

        def substitute(eng, own, d, steps):
            for k in steps:
                col, row, dst, term = substitution(k, d)
                own.done(eng.tensor_tensor(term, col.to_broadcast(term.shape), row.to_broadcast(term.shape), ALU.mult))
                own.done(eng.tensor_tensor(dst, dst, term, ALU.subtract))

        def bank(b, n=T):
            return ps[:, b, 0:n]

        def quads(b):
            return ps[:, b, :].rearrange("p (c d) -> p c d", d=P)

        rows_loaded, consts_loaded = sem("rows_loaded"), sem("consts_loaded")
        x_loaded = [sem(f"x_loaded{b}") for b in range(2)]
        setup_turned, x_turned, x_evacuated = sem("setup_turned"), sem("x_turned"), sem("x_evacuated")
        staged, c_ready, x_stored, lam_exp = sem("staged"), sem("c_ready"), sem("x_stored"), sem("lam_exp")
        masks_loaded = sem("masks_loaded")
        x_measured = sem("x_measured")
        w_loaded = [sem(f"w_loaded{s}") for s in range(4)]
        w_hi_ready, w_split, w_used = sem("w_hi_ready"), sem("w_split"), sem("w_used")
        ada_loaded = [sem(f"ada_loaded{s}") for s in range(6)]
        ada_used, ada_copied = sem("ada_used"), sem("ada_copied")
        ada_turned, mod_ready = sem("ada_turned"), sem("mod_ready")
        sums_ready, sums_turned, sums_copied = sem("sums_ready"), sem("sums_turned"), sem("sums_copied")
        rms_ready, diag_ready, rms_spread, rms_copied = sem("rms_ready"), sem("diag_ready"), sem("rms_spread"), sem("rms_copied")
        x_scaled, h_hi_ready, h_ready = sem("x_scaled"), sem("h_hi_ready"), sem("h_ready")
        evacuated = sem("evacuated")
        conv_done, tanh_done, qkv_ready = sem("conv_done"), sem("tanh_done"), sem("qkv_ready")
        rot_done, rope_done = sem("rot_done"), sem("rope_done")
        z_tanh, z_ready = sem("z_tanh"), sem("z_ready")
        ab_turned, ab_exp, tab_g, tab_beta, tab_sums = sem("ab_turned"), sem("ab_exp"), sem("tab_g"), sem("tab_beta"), sem("tab_sums")
        tab_ready, tab_abs, tab_soft, tab_last, tab_rows = sem("tab_ready"), sem("tab_abs"), sem("tab_soft"), sem("tab_last"), sem("tab_rows")
        rows_copied, rows_stored, g_loaded = sem("rows_copied"), sem("rows_stored"), sem("g_loaded")
        decay_arg, decay_ready = sem("decay_arg"), sem("decay_ready")
        qk_turned, v_turned, qk_squared, qk_summed, qk_rms = sem("qk_turned"), sem("v_turned"), sem("qk_squared"), sem("qk_summed"), sem("qk_rms")
        vb_ready, qk_normed, qk_returned, qk_T_ready, grams = sem("vb_ready"), sem("qk_normed"), sem("qk_returned"), sem("qk_T_ready"), sem("grams")
        k_scaled, inv_turned = sem("k_scaled"), sem("inv_turned")
        m_ready, blocks_out, blocks_in = sem("m_ready"), sem("blocks_out"), sem("blocks_in")
        zeros_set, zeros_out, blk_identity = sem("zeros_set"), sem("zeros_out"), sem("blk_identity")
        blocks_solved, solved_out, inv_started = sem("blocks_solved"), sem("solved_out"), sem("inv_started")
        x_product = [sem(f"x_product{d}") for d in range(2)]
        x_masked = [sem(f"x_masked{d}") for d in range(2)]
        t_product = [sem(f"t_product{d}") for d in range(2)]
        t_merged = [sem(f"t_merged{d}") for d in range(2)]
        q_decayed, w_product, w_ready = sem("q_decayed"), sem("w_product"), sem("w_ready")
        v_product, v_ready, s_product, s_ready = sem("v_product"), sem("v_ready"), sem("s_product"), sem("s_ready")
        ob_product, ob_squared, ob_summed, ob_rms, ob_normed = sem("ob_product"), sem("ob_squared"), sem("ob_summed"), sem("ob_rms"), sem("ob_normed")
        ob_turned, yb_ready, yb_stored = sem("ob_turned"), sem("yb_ready"), sem("yb_stored")
        va_turned, va_ready, scored, maxed, exped, mixed = sem("va_turned"), sem("va_ready"), sem("scored"), sem("maxed"), sem("exped"), sem("mixed")
        p_turned, p_copied, oa_product, oa_copied = sem("p_turned"), sem("p_copied"), sem("oa_product"), sem("oa_copied")
        oa_squared, oa_summed, oa_rms, oa_normed = sem("oa_squared"), sem("oa_summed"), sem("oa_rms"), sem("oa_normed")
        oa_turned, ya_ready, ya_stored = sem("oa_turned"), sem("ya_ready"), sem("ya_stored")
        y_loaded = [sem(f"y_loaded{g}") for g in range(4)]
        y_hi_ready, y_split, out_added = sem("y_hi_ready"), sem("y_split"), sem("out_added")
        last_product = sem("last_product")
        part_loaded = [sem(f"part_loaded{b}") for b in range(2)]
        part_stored = [sem(f"part_stored{b}") for b in range(2)]
        old_loaded = [sem(f"old_loaded{g}") for g in range(4)]
        x_squared, x_scratch = sem("x_squared"), sem("x_scratch")
        fin_scaled, fin_turned, fin_copied, fin_stored = sem("fin_scaled"), sem("fin_turned"), sem("fin_copied"), sem("fin_stored")
        vec_step, act_step, sp_step, pool_step = sem("vec_step"), sem("act_step"), sem("sp_step"), sem("pool_step")

        def first_q(layer):
            return 0 if layer < DEPTH - 1 else N_CTX // P

        def tokens(layer, tile):
            return 0 if tile in (BK, BV, AK, AV) else first_q(layer) * P

        LAYER_UNITS = 2 + HEADS * UNITS + OUT_UNITS + LAST_UNITS
        ALL_UNITS = DEPTH * LAYER_UNITS
        LAYER_TILES = 1 + HEADS * TILES
        ADA_START = 2 * KT
        ADA_IN = {0: 6, 1: 2}

        RING = 6
        last_use = [max(u for u in range(2 * ADA_START) if u % RING == s) for s in range(RING)]

        def group_block(g):
            return (g % 2) * KT + 4 * (g // 2)

        def modulated_after(g):
            return {2: 0, 3: 1, 5: 2, 7: 3}.get(g, -1)

        def ada_block(layer, k):
            return [(0, 2 * KT), (1, 0), (1, KT)][k // 2] if layer == 0 else (1, 2 * KT)

        def ada_before(layer):
            return ADA_START + (0 if layer == 0 else HEADS * ADA_IN[0])

        def nth(layer, i, off, per=1, idx=1):
            return i * per + (HEADS * layer + off) * per + idx

        LVL = len(LEVELS)
        Y_GROUPS = (slice(0, 4), slice(4, 7), slice(8, 12), slice(12, 15))
        Y_STEPS = len(Y_GROUPS) + 2
        y_group_of = {k: g for g, ks in enumerate(Y_GROUPS) for k in range(ks.start, ks.stop)}

        def piece_slot(p):
            return 8 + p * (SLOTS - 8) // (2 * OUT_UNITS)

        def out_slot(n):
            return min(piece_slot(4 * n + 3) + 1, SLOTS - 1)
        q_tiles = {0: (2, 3, 0, 1), 1: (2, 3)}
        QT_BEFORE = {0: 0, 1: HEADS * 4}

        def nth_q(layer, i, off, idx):
            per = len(q_tiles[layer])
            return i * per + (QT_BEFORE[layer] + off * per + idx)

        ORDER = ((0, 1, 2, 3), (1, 0, 3, 2))

        block = ctx.enter_context(nc.Block())

        def heads(eng, layer, body):
            body(0, True, False)
            if layer == 0:
                body(1, True, True)
            with eng.Fori(2 if layer == 0 else 1, HEADS) as i:
                body(i, True, True)
            body(HEADS, False, True)

        @block.sync
        def _(sp):
            sp.dma_start(cst[:], consts).then_inc(consts_loaded, 16)
            sp.wait_ge(staged, 1)
            sp.dma_start(rows_in[0:16, 0], c_ctx.rearrange("(k p) -> k p", p=P)).then_inc(rows_loaded, 16)
            sp.dma_start(rows_in[16:32, 0], c.rearrange("b (k p) -> (b k) p", p=P)).then_inc(rows_loaded, 16)
            sp.dma_start(rows_in[32:64, 0], norm_w.rearrange("l (k p) -> (l k) p", p=P)).then_inc(rows_loaded, 16)
            sp.dma_start(rows_in[64:80, 0], final_norm_w.rearrange("(k p) -> k p", p=P)).then_inc(rows_loaded, 16)
            sp.dma_start(rows_in[80:82, 0], dn_norm_w).then_inc(rows_loaded, 16)
            sp.dma_start(rows_in[82:84, 0], subln_w).then_inc(rows_loaded, 16)
            sp.dma_start(rows_in[0:96, 1], b_ada.rearrange("l (k p) -> (l k) p", p=P)).then_inc(rows_loaded, 16)
            for l in range(DEPTH):
                sp.dma_start(rows_in[0:120, 2 + l],
                             conv_w[l].rearrange("j (k p) -> (j k) p", p=P)).then_inc(rows_loaded, 16)
            sp.dma_start(lam_in, diff_lambda.rearrange("l a d -> (l a d)").unsqueeze(0)
                         .to_broadcast([P, DEPTH * 4 * 64])).then_inc(rows_loaded, 16)
            for n, v in enumerate((dn_a_log, dn_dt_bias)):
                sp.dma_start(alog[:, n].rearrange("p l h -> p (l h)"),
                             v.rearrange("l a h -> (l a h)").unsqueeze(0)
                             .to_broadcast([P, DEPTH * 2 * HEADS])).then_inc(rows_loaded, 16)

            def load_x(n):
                if n >= 2:
                    sp.wait_ge(x_turned, (n - 1) * 4)
                sp.dma_start(x_in[:, n % 2], toks[n // 2][(n % 2) * P:(n % 2 + 1) * P, :]).then_inc(x_loaded[n % 2], 16)

            def ada_columns(layer, block_, half):
                return w_ada[layer].rearrange("(k p) n -> p k n", p=P)[:, half * HALF:(half + 1) * HALF,
                                                                      bass.ds(block_ * P, P)]

            load_x(0)
            load_x(1)
            for u in range(2 * ADA_START):
                group, pair = u // 8, u % 8
                if u in (RING - 2, RING):
                    n = 2 if u < RING else 3
                    sp.wait_ge(x_measured, n - 1)
                    load_x(n)
                if u >= RING:
                    sp.wait_ge(ada_used, u - RING + 1)
                sp.dma_start(ada_ring[u % RING].rearrange("p k n -> p (k n)").rearrange("p (k n) -> p k n", k=2),
                             w_ada[0].rearrange("(k p) n -> p k n", p=P)[
                                 :, 2 * pair:2 * pair + 2, group_block(group) * P:(group_block(group) + 4) * P]
                             ).then_inc(ada_loaded[u % RING], 16)

            def w_unit(i, u, source, tiles=HALF):
                s = u % 4
                if isinstance(i, int) and i * UNITS + u < 4:
                    sp.wait_ge(ada_used, last_use[s] + 1)
                else:
                    sp.wait_ge(w_split, i * UNITS + (u - 3))
                    sp.sem_inc(sp_step, 1)
                dst = w_raw[:, s, 0:tiles]
                if source.shape[-1] == T:
                    dst = dst.rearrange("p k n -> p (k n)").rearrange("p (k n) -> p k n", n=T)
                sp.dma_start(dst, source).then_inc(w_loaded[s], 16)

            def ada_unit(layer, i, k, half):
                lay, first = ada_block(layer, k)
                n = i * (2 * ADA_IN[layer]) + (ada_before(layer) * 2 + 2 * k + half)
                sp.wait_ge(ada_used, n - 1)
                sp.sem_inc(sp_step, 1)
                sp.dma_start(ada_raw[:, half], ada_columns(lay, i * 2 + (first + k % 2), half)).then_inc(
                    ada_loaded[4 + half], 16)

            for layer in range(DEPTH):
                base = layer * LAYER_UNITS
                c0 = first_q(layer)
                w_cols = w_in[layer].rearrange("(k p) n -> p k n", p=P)
                for half in range(2):
                    w_unit(0, base + half, w_cols[:, half * HALF:(half + 1) * HALF, N_IN - P:N_IN])

                def blocks_to_partitions(i):
                    sp.wait_ge(m_ready, nth(layer, i, -1))
                    sp.dma_start(chunk_rows(m_dram), m_T.rearrange("p x c d -> p (x c) d")).then_inc(blocks_out, 16)
                    sp.wait_ge(blocks_out, nth(layer, i, -1, 16, 16))
                    sp.dma_start(sub(blk_m), diagonal_blocks(m_dram)).then_inc(blocks_in, 16)

                def blocks_back(i):
                    sp.wait_ge(blocks_solved, nth(layer, i, -1, 2, 2))
                    sp.dma_start(diagonal_blocks(s_dram), sub(blk_s)).then_inc(solved_out, 16)
                    sp.wait_ge(solved_out, nth(layer, i, -1, 16, 16))
                    sp.dma_start(inv_T.rearrange("p x c d -> p (x c) d"), chunk_rows(s_dram)).then_inc(inv_started, 16)

                wo = w_out[layer].rearrange("(k p) n -> p k n", p=P)
                first = base + 2 + HEADS * UNITS

                def output_part():
                    for u in range(OUT_UNITS):
                        half, n = u % 2, u // 2
                        ks = slice(half * HALF, half * HALF + OUT_HEADS)
                        w_unit(0, first + u, wo[:, ks, n * P:(n + 1) * P], OUT_HEADS)
                        if u == 3:
                            sp.wait_ge(w_used, first)
                            sp.wait_ge(ya_stored, 16 * (HEADS * layer + OUT_HEADS))
                            sp.wait_ge(yb_stored, 16 * (HEADS * layer + OUT_HEADS))
                            for g, ks in enumerate(Y_GROUPS):
                                sp.dma_start(h_lo[:, ks, c0 * P:].bitcast(F32),
                                             y_dram[layer, ks, :, c0 * P:].rearrange("k p t -> p k t")).then_inc(y_loaded[g], 16)
                        if u == 7:
                            blocks_to_partitions(HEADS)
                        if u == 11:
                            blocks_back(HEADS)

                def body(i, project, fill):
                    if not project:
                        output_part()
                        return
                    for k in range(UNITS):
                        t, half = k // 2, k % 2
                        if fill and k == 8:
                            blocks_to_partitions(i)
                        if fill and k == 10:
                            blocks_back(i)
                        w_unit(i, base + 2 + k,
                               w_cols[:, half * HALF:(half + 1) * HALF, bass.ds(i * P + COLUMN[t], P)])
                        if k >= 10 and k - 10 < ADA_IN[layer]:
                            for hf in range(2):
                                ada_unit(layer, i, k - 10, hf)
                heads(sp, layer, body)
                for u in range(LAST_UNITS):
                    w_unit(0, first + OUT_UNITS + u, wo[:, OUT_HEADS::HEADS, u * T:(u + 1) * T])

        @block.scalar
        def _(act):
            own = Count(act, act_step)

            def split_hi(i, u, tiles=HALF):
                s = u % 4
                act.wait_ge(w_loaded[s], i * (16 * UNITS // 4) + 16 * (u // 4 + 1))
                need(act, w_used, i * UNITS + (u - 1))
                nc.scalar.copy(w_hi[:, u % 2, 0:tiles], w_raw[:, s, 0:tiles]).then_inc(w_hi_ready, 1)

            act.wait_ge(setup_turned, 1)
            own.done(nc.scalar.copy(vecs[:].rearrange("p b n -> p (b n)"), bank(A0)))
            nc.scalar.activation(small[:, 0:2 * KT], vecs[:, 0, 0:2 * KT], ACT.Tanh, scale=0.5).then_inc(c_ready, 1)
            act.wait_ge(c_ready, 1)
            act.wait_ge(staged, 3)
            nc.scalar.activation(small[:, 40:44], small[:, 40:44], ACT.Exp).then_inc(lam_exp, 1)

            def copy_x(n, q):
                act.wait_ge(x_turned, n * 4 + q + 1)
                nc.scalar.copy(xT[:, 4 * q:4 * q + 4, n * P:(n + 1) * P], quads(G0 + q)).then_inc(x_evacuated, 1)
                act.wait_ge(x_evacuated, n * 4 + q + 1)

            def ada_copy(value):
                act.wait_ge(ada_used, value * 2)
                need(act, ada_turned, value - 1)
                nc.scalar.copy(ada_sb[:], bank(A0, P)).then_inc(ada_copied, 1)
                act.wait_ge(ada_copied, value)

            def measure_x(n):
                act.wait_ge(x_loaded[n % 2], 16 * (n // 2 + 1))
                nc.scalar.activation(x_squares, x_in[:, n % 2], ACT.Square, accum_out=small[:, 44 + n:45 + n]).then_inc(x_measured, 1)
                act.wait_ge(x_measured, n + 1)

            def copy_rms(layer, bank_):
                act.wait_ge(rms_spread, layer + 1)
                nc.scalar.copy(x_rms, bank(bank_)).then_inc(rms_copied, 1)
                act.wait_ge(rms_copied, layer + 1)

            def modulate(layer, ks):
                for k in ks:
                    act.wait_ge(x_scaled, layer * KT + k + 1)
                    for v in range(2):
                        seg = slice(v * N_CTX, (v + 1) * N_CTX)
                        own.go(nc.scalar.activation(h_tmp[:, k % 2, seg], h_tmp[:, k % 2, seg], ACT.Identity,
                                                    scale=scale_w[:, k, v:v + 1], bias=mod[:, layer, k, v:v + 1]))
                    own.settle()
                    nc.scalar.copy(h_hi[:, k], h_tmp[:, k % 2]).then_inc(h_hi_ready, 1)
                    act.wait_ge(h_hi_ready, layer * KT + k + 1)

            for n in range(2):
                measure_x(n)
                for q in range(4):
                    copy_x(n, q)
            for g in range(ADA_START // 4):
                act.wait_ge(ada_used, 8 * (g + 1))
                if g >= 2:
                    act.wait_ge(ada_turned, 4 * (g - 1))
                nc.scalar.copy(ada_wide[:, g % 2], bank(A0)).then_inc(ada_copied, 4)
                act.wait_ge(ada_copied, 4 * (g + 1))
                if g < 2:
                    measure_x(2 + g)
                    for q in range(4):
                        copy_x(2 + g, q)
                if g == 2:
                    copy_rms(0, G1)
                if g == 7:
                    act.dma_start(x_dram.rearrange("k p t -> p k t"), xT).then_inc(x_stored, 16)
                if g == 7:
                    split_hi(0, 0)
                q = modulated_after(g)
                if q >= 0:
                    modulate(0, range(4 * q, 4 * q + 4))

            for layer in range(DEPTH):
                base = layer * LAYER_UNITS
                c0 = first_q(layer)
                own.finish()
                if layer:
                    split_hi(0, base)
                    copy_rms(layer, A1)
                    modulate(layer, range(HALF))
                    split_hi(0, base + 1)
                    modulate(layer, range(HALF, KT))
                else:
                    split_hi(0, base + 1)
                split_hi(0, base + 2)

                def tile_count(i, off, t):
                    return i * TILES + (layer * LAYER_TILES + 1 + off * TILES + t + 1)

                act.wait_ge(w_used, base + 2)
                act.wait_ge(x_stored, 16 * (1 + layer * KT))
                nc.scalar.copy(th[96:128], ps[96:128, PJ + 0, :]).then_inc(evacuated, 1)
                act.wait_ge(evacuated, layer * LAYER_TILES + 1)

                def table_step(s):
                    gx = decay[:, 0, 0, 0:NT * 16].rearrange("p (c n) -> p c n", c=NT)
                    e = decay[:, 0, 1, 0:NT * 16].rearrange("p (c n) -> p c n", c=NT)
                    tb = decay[:, 0, 2, 0:NT * 16].rearrange("p (c n) -> p c n", c=NT)
                    raw = bank(A0, P).rearrange("p (c n) -> p c n", c=NT)
                    if s == 0:
                        act.wait_ge(tab_g, layer + 1)
                        own.done(nc.scalar.activation(e, gx, ACT.Abs))
                        own.done(nc.scalar.activation(tb, raw[:, :, 16:32], ACT.Tanh, scale=0.5))
                        own.done(nc.scalar.activation(small[:, 48:64], alog[:, 0, layer], ACT.Exp))
                        own.done(nc.scalar.activation(e, e, ACT.Exp, scale=-1.0))
                        nc.scalar.activation(e, e, ACT.Ln, bias=1.0).then_inc(tab_soft, 1)
                        act.wait_ge(tab_soft, layer + 1)
                    if s == 1:
                        act.wait_ge(tab_last, layer + 1)
                        tabf = tab[:].rearrange("p k x c h -> p k (x c h)")
                        own.go(nc.scalar.activation(tabf[:, TAB_GROW], bank(A1, 64), ACT.Exp))
                        own.go(nc.scalar.activation(tabf[:, TAB_LAST], ps[:, A1, 64:128], ACT.Exp))
                        nc.scalar.activation(tabf[:, TAB_END], decay[:, 0, 3, 0:64], ACT.Exp).then_inc(tab_ready, 1)
                        act.wait_ge(tab_ready, layer + 1)
                        own.settle()
                    if s == 2:
                        act.wait_ge(tab_rows, layer + 1)
                        nc.scalar.copy(sq_b[0:16, 0:4, :].rearrange("p c d -> p (c d)"), ps[0:16, A0, :]).then_inc(rows_copied, 1)
                        act.wait_ge(rows_copied, layer + 1)
                        act.dma_start(g_dram[layer], sq_b[0:16, 0:4, :].rearrange("p c d -> p (c d)")).then_inc(rows_stored, 16)
                        act.wait_ge(rows_stored, 16 * (layer + 1))

                def load_g(i, off):
                    rows = g_dram[layer].rearrange("(x h) t -> x h t", h=HEADS)[:, bass.ds(i + off, 1), :]
                    act.dma_start(g_row.rearrange("p x c d -> p x (c d)"),
                                  rows.rearrange("x o t -> o x t").to_broadcast([P, 2, T])).then_inc(g_loaded, 16)

                def body(i, project, fill):
                    own.finish()

                    def h(off=-1, per=1, idx=1):
                        return nth(layer, i, off, per, idx)

                    def evacuate(t):
                        src = bank(PJ + (1 + t) % 2)
                        q0 = tokens(layer, t)
                        act.wait_ge(w_used, i * UNITS + (base + 2 + 2 * t + 2))
                        val = tile_count(i, 0, t)
                        if t in (BQ, BK, BV):
                            need(act, conv_done, nth(layer, i, 0, 3, t))
                            s0 = q0 // N_CTX
                            nc.scalar.copy(cin[:, s0:, PAD:PAD + N_CTX],
                                           src.rearrange("p (s n) -> p s n", s=2)[:, s0:]).then_inc(evacuated, 1)
                        elif t in (AK, AQ):
                            need(act, scored, nth_q(layer, i, 0, 0))
                            need(act, rope_done, nth(layer, i, 0, 2, 0 if t == AK else 1))
                            if q0 == 0:
                                own.go(nc.scalar.copy((a_k if t == AK else a_q)[:, 0:N_CTX], src[:, 0:N_CTX]))
                            nc.scalar.copy(a_raw, src[:, N_CTX:T]).then_inc(evacuated, 1)
                            own.settle()
                        elif t == AV:
                            need(act, va_turned, h(-1))
                            nc.scalar.copy(a_v, src).then_inc(evacuated, 1)
                        act.wait_ge(evacuated, val)

                    def evacuate_z(off, t):
                        src = bank(PJ + (1 + t) % 2)
                        z = z_a if t == ZA else z_b
                        q0 = tokens(layer, t)
                        act.wait_ge(w_used, i * UNITS + (base + 2 + off * UNITS + 2 * t + 2))
                        if t == ZA:
                            need(act, ya_ready, nth(layer, i, off, 1, 0))
                            need(act, z_ready, nth(layer, i, off, 2, 0))
                        else:
                            need(act, yb_ready, nth(layer, i, off, 1, 0))
                            act.wait_ge(z_ready, nth(layer, i, off, 2, 1))
                        own.go(nc.scalar.activation(th_z[:, q0:], src[:, q0:], ACT.Tanh, scale=0.5))
                        nc.scalar.copy(z[:, q0:], src[:, q0:]).then_inc(evacuated, 1)
                        own.settle()
                        act.wait_ge(evacuated, tile_count(i, off, t))

                    def tanh(x_):
                        act.wait_ge(conv_done, nth(layer, i, 0, 3, x_ + 1))
                        q0 = tokens(layer, x_)
                        nc.scalar.activation(th[:, q0:], qkv[:, x_, q0:], ACT.Tanh, scale=0.5).then_inc(tanh_done, 1)
                        act.wait_ge(tanh_done, nth(layer, i, 0, 3, x_ + 1))

                    def squares():
                        act.wait_ge(qk_turned, h())
                        flat = ps[:, G0:G0 + 2, :].rearrange("p b (c d) -> p (b c) d", d=P)
                        nc.scalar.activation(sq_b[:, c0:], flat[:, c0:], ACT.Square).then_inc(qk_squared, 1)
                        act.wait_ge(qk_squared, h())

                    def v_copy():
                        act.wait_ge(v_turned, h())
                        nc.scalar.activation(v_tok.rearrange("p c d -> p (c d)"), bank(G2), ACT.Copy, scale=0.5).then_inc(vb_ready, 1)
                        act.wait_ge(vb_ready, h())

                    def decays():
                        act.wait_ge(decay_arg, h())
                        need(act, ob_turned, h(-2))
                        own.go(nc.scalar.activation(q_dec[:, :, c0:], g_row[:, :, c0:], ACT.Exp))
                        nc.scalar.activation(decay, decay, ACT.Exp).then_inc(decay_ready, 1)
                        act.wait_ge(decay_ready, h())
                        own.settle()
                        if not (isinstance(i, int) and i == HEADS):
                            load_g(i, 0)

                    def qk_copy():
                        act.wait_ge(qk_returned, h())
                        flat = ps[:, G0:G0 + 2, :].rearrange("p b (c d) -> p (b c) d", d=P)
                        nc.scalar.copy(qk_T[:, c0:], flat[:, c0:]).then_inc(qk_T_ready, 1)
                        act.wait_ge(qk_T_ready, h())

                    def w_copy(d):
                        act.wait_ge(w_product, h(-1, 2, d + 1))
                        nc.scalar.activation(w_T[:, d], quads(GX[d]), ACT.Copy, scale=-1.0).then_inc(w_ready, 1)
                        act.wait_ge(w_ready, h(-1, 2, d + 1))

                    def v_new_copy(j):
                        act.wait_ge(v_product, h(-1, 4, j + 1))
                        for d in range(2):
                            ch = ORDER[d][j]
                            m = nc.scalar.activation(v_new[:, d, ch], ps[:, GT[d], 0:P], ACT.Copy,
                                                     scale=hcol[:, TAB_BETA, d, ch:ch + 1])
                            if d == 0:
                                own.go(m)
                        m.then_inc(v_ready, 1)
                        own.settle()
                        act.wait_ge(v_ready, h(-1, 4, j + 1))

                    def o_squares():
                        act.wait_ge(ob_product, h())
                        nc.scalar.activation(sq_b[:, c0:NT], quads(G0)[:, c0:], ACT.Square).then_inc(ob_squared, 1)
                        act.wait_ge(ob_squared, h())

                    def y_store(which):
                        yy, ready, stored = ((y_a, ya_ready, ya_stored), (y_b, yb_ready, yb_stored))[which]
                        act.wait_ge(ready, h())
                        act.dma_start(y_dram[layer][bass.ds(i + (HEADS * which - 1), 1), :, c0 * P:].rearrange("o p t -> (o p) t"),
                                      yy[:, c0 * P:]).then_inc(stored, 16)

                    def va_copy():
                        act.wait_ge(va_turned, h())
                        nc.scalar.copy(va_tok, quads(A0)).then_inc(va_ready, 1)
                        act.wait_ge(va_ready, h())

                    def exps(n):
                        qt = q_tiles[layer][n]
                        keys = T if qt >= 2 else N_CTX
                        act.wait_ge(maxed, nth_q(layer, i, -1, n + 1))
                        for m in range(2):
                            last = nc.scalar.activation(prob[:, m, 0:keys], bank(A0 + m, keys), ACT.Exp, scale=0.125,
                                                        bias=small[:, 34 + m:35 + m], accum_out=small[:, 36 + m:37 + m])
                            if m == 0:
                                own.go(last)
                        last.then_inc(exped, 1)
                        own.settle()
                        act.wait_ge(exped, nth_q(layer, i, -1, n + 1))

                    def p_copy(n):
                        qt = q_tiles[layer][n]
                        kt = NT if qt >= 2 else 2
                        act.wait_ge(p_turned, nth_q(layer, i, -1, n + 1))
                        nc.scalar.copy(prob_T[:, 0:kt], quads(A0)[:, 0:kt]).then_inc(p_copied, 1)
                        act.wait_ge(p_copied, nth_q(layer, i, -1, n + 1))

                    def oa_copy(n):
                        act.wait_ge(oa_product, nth_q(layer, i, -1, n + 1))
                        nc.scalar.copy(o_a[:, q_tiles[layer][n]], bank(A1, P)).then_inc(oa_copied, 1)
                        act.wait_ge(oa_copied, nth_q(layer, i, -1, n + 1))

                    def oa_squares():
                        nc.scalar.activation(sq_a[:, 0, c0 * P:], o_a[:, c0:].rearrange("p c d -> p (c d)"),
                                             ACT.Square).then_inc(oa_squared, 1)
                        act.wait_ge(oa_squared, h())

                    def ada(k):
                        ada_copy(i * ADA_IN[layer] + (ada_before(layer) + k + 1))

                    def y_hi(g):
                        act.wait_ge(y_loaded[g], 16 * (layer + 1))
                        ks = Y_GROUPS[g]
                        nc.scalar.copy(h_hi[:, ks, c0 * P:], h_lo[:, ks, c0 * P:].bitcast(F32)).then_inc(y_hi_ready, 1)
                        act.wait_ge(y_hi_ready, layer * Y_STEPS + g + 1)

                    def y_hi_last(which):
                        nc.scalar.copy(h_hi[:, OUT_HEADS + HEADS * which, c0 * P:],
                                       (y_a, y_b)[which][:, c0 * P:]).then_inc(y_hi_ready, 1)
                        act.wait_ge(y_hi_ready, layer * Y_STEPS + len(Y_GROUPS) + which + 1)

                    def part_load(n):
                        if n == 0:
                            act.wait_ge(qkv_ready, h(-1, 3, 3))
                            act.wait_ge(x_stored, 16 * (1 + layer * KT))
                        if n >= 2:
                            act.wait_ge(part_stored[n % 2], 16 * (layer * KT // 2 + n // 2))
                        act.dma_start(x_part[n % 2][:, c0 * P:], x_dram[n, :, c0 * P:]).then_inc(part_loaded[n % 2], 16)

                    def part_store(n):
                        act.wait_ge(out_added, layer * 2 * KT + n + 1)
                        act.dma_start(x_dram[n, :, c0 * P:], x_part[n % 2][:, c0 * P:]).then_inc(part_stored[n % 2], 16)

                    plan = {}

                    def put(s, f, *a):
                        plan.setdefault(s, []).append((f, a))

                    if not project:
                        put(2, part_load, 0)
                        put(2, part_load, 1)
                        for g in range(len(Y_GROUPS)):
                            put((3, 4, 6, 7)[g], y_hi, g)
                        put(40, y_hi_last, 0)
                    if fill:
                        put(0, evacuate_z, -1, ZB)
                        put(0, va_copy)
                        put(1, squares)
                        put(1, v_copy)
                        put(3, decays)
                        put(6, qk_copy)
                        put(39, w_copy, 0)
                        put(40, w_copy, 1)
                        for j in range(4):
                            put(42 + 4 * j, v_new_copy, j)
                        put(57, o_squares)
                        put(62, y_store, 1)
                        for n in range(len(q_tiles[layer])):
                            put(3 + 8 * n, exps, n)
                            put(7 + 8 * n, p_copy, n)
                            put(9 + 8 * n, oa_copy, n)
                        put(3 + 8 * len(q_tiles[layer]), oa_squares)
                        put(39, y_store, 0)
                    if project:
                        for t in (BQ, BK, BV, AK, AV, AQ):
                            put(8 * t + 8, evacuate, t)
                        for x_ in range(3):
                            put(8 * x_ + 14, tanh, x_)
                        put(56, evacuate_z, 0, ZA)
                        for k in range(ADA_IN[layer]):
                            put(43 + 3 * k, ada, k)
                        if isinstance(i, int) and i == 0:
                            put(3, table_step, 0)
                            put(6, table_step, 1)
                            put(8, table_step, 2)
                            put(12, load_g, 0, 0)
                    if not project:
                        put(62, y_hi_last, 1)
                        for n in range(KT):
                            put(out_slot(n), part_store, n)
                            if n + 2 < KT:
                                put(min(out_slot(n) + 2, SLOTS - 1), part_load, n + 2)
                        for u in range(OUT_UNITS):
                            put(piece_slot(2 * u), split_hi, 0, first + u + 1, OUT_HEADS if u < OUT_UNITS - 1 else HALF)
                    for s in range(SLOTS):
                        if project and s % 4 == 1:
                            split_hi(i, base + 2 + s // 4 + 1)
                        for f, a in plan.get(s, ()):
                            f(*a)
                    own.finish()

                first = base + 2 + HEADS * UNITS

                own.finish()
                heads(act, layer, body)

                own.finish()
                act.wait_ge(yb_ready, HEADS * (layer + 1))
                for stored in (ya_stored, yb_stored):
                    act.wait_ge(stored, 16 * HEADS * (layer + 1))
                for b in range(2):
                    act.wait_ge(part_stored[b], 16 * (layer + 1) * KT // 2)
                act.wait_ge(y_split, Y_STEPS * (layer + 1))
                for g in range(4):
                    ks = slice(4 * g, 4 * g + 4)
                    act.dma_start(xT[:, ks, c0 * P:], x_dram[ks, :, c0 * P:].rearrange("k p t -> p k t")).then_inc(old_loaded[g], 16)
                for n in range(KT):
                    if n % 4 == 0 and n // 4 + 1 < LAST_UNITS:
                        split_hi(0, first + OUT_UNITS + n // 4 + 1)
                    act.wait_ge(out_added, (2 * layer + 1) * KT + n + 1)
                    need(act, sums_ready, layer * KT + n - 1)
                    nc.scalar.activation(sq_tiles[n % 2][:, c0 * P:], xT[:, n, c0 * P:], ACT.Square).then_inc(x_squared, 1)
                    act.wait_ge(x_squared, layer * KT + n + 1)
                    if layer == 0:
                        act.dma_start(x_dram[n, :, N_CTX:], xT[:, n, N_CTX:]).then_inc(x_stored, 16)

            act.wait_ge(rms_spread, DEPTH + 1)
            nc.scalar.copy(x_rms[:, N_CTX:], ps[:, A1, N_CTX:]).then_inc(rms_copied, 1)
            act.wait_ge(rms_copied, DEPTH + 1)
            for n in range(2):
                for q in range(4):
                    act.wait_ge(fin_turned, n * 4 + q + 1)
                    nc.scalar.copy(o_row[:, n, q * T:(q + 1) * T], bank(G0 + q)).then_inc(fin_copied, 1)
                    act.wait_ge(fin_copied, n * 4 + q + 1)
                act.dma_start(out2[n * P:(n + 1) * P, :], o_row[:, n]).then_inc(fin_stored, 16)
            act.wait_ge(fin_stored, 32)
            act.wait_ge(x_stored, 16 * (1 + KT))
            act.wait_ge(ya_stored, 16 * DEPTH * HEADS)
            act.wait_ge(yb_stored, 16 * DEPTH * HEADS)

        @block.vector
        def _(vec):
            own = Count(vec, vec_step)
            V = nc.vector

            def tt(o, a, b, op):
                return V.tensor_tensor(o, a, b, op)

            own.go(V.memset(rows_in, 0.0))
            own.go(V.memset(c_T[:], 0.0))
            own.go(V.memset(minus_half[:], -0.5))
            V.memset(sq_sum, 0.0).then_inc(staged, 1)
            vec.wait_ge(staged, 1)
            own.settle()
            vec.wait_ge(masks_loaded, 16)
            vec.wait_ge(consts_loaded, 16)
            vec.wait_ge(c_ready, 1)
            own.done(V.tensor_scalar(small[:, 0:2 * KT], small[:, 0:2 * KT], 1.0, 0.5, ALU.add, ALU.mult))
            tt(c_T[:, :, 0:2].rearrange("p k v -> p v k"), small[:, 0:2 * KT].rearrange("p (v k) -> p v k", v=2),
               vecs[:, 0, 0:2 * KT].rearrange("p (v k) -> p v k", v=2), ALU.mult).then_inc(staged, 1)
            vec.wait_ge(staged, 2)
            vec.wait_ge(rows_loaded, 16 * 12)
            lv = lam_in.rearrange("p (l a d) -> p l a d", l=DEPTH, a=4)
            own.done(tt(lv[:, :, 0::2, :], lv[:, :, 0::2, :], lv[:, :, 1::2, :], ALU.mult))
            V.tensor_reduce(small[:, 40:44].rearrange("p (l a) -> p l a", l=DEPTH), lv[:, :, 0::2, :], AX, ALU.add).then_inc(staged, 1)
            vec.wait_ge(staged, 3)

            def mod_column(value, lay, blk):
                vec.wait_ge(ada_turned, value)
                tt(mod[:, lay, bass.ds(blk, 1), :].rearrange("p o v -> p (o v)"), bank(A1, 2),
                   vecs[:, 1, bass.ds(blk + lay * 3 * KT, 1)].to_broadcast([P, 2]), ALU.add).then_inc(mod_ready, 1)
                vec.wait_ge(mod_ready, value)

            def rms(n, c0):
                if n:
                    vec.wait_ge(sums_turned, n)
                    V.tensor_copy(small[:, 44 + c0:48], ps[:, A0, c0:NT]).then_inc(sums_copied, 1)
                    vec.wait_ge(sums_copied, n)
                vec.wait_ge(rms_ready, n + 1)
                for cc in range(c0, NT):
                    m = V.tensor_scalar(diag[:, cc * P:(cc + 1) * P], ident, small[:, 44 + cc:45 + cc], None, ALU.mult)
                    if cc < NT - 1:
                        own.go(m)
                m.then_inc(diag_ready, 1)
                vec.wait_ge(diag_ready, n + 1)
                own.settle()

            def split_lo(i, u, tiles=HALF):
                vec.wait_ge(w_hi_ready, i * UNITS + (u + 1))
                need(vec, w_used, i * UNITS + (u - 1))
                tt(w_lo[:, u % 2, 0:tiles], w_raw[:, u % 4, 0:tiles], w_hi[:, u % 2, 0:tiles].bitcast(F32),
                   ALU.subtract).then_inc(w_split, 1)

            def modulate(layer, ks):
                n = 32 + 16 * layer
                own.done(V.scalar_tensor_tensor(
                    scale_w[:, ks.start:ks.stop], mod[:, layer, KT + ks.start:KT + ks.stop, :], 1.0,
                    vecs[:, 0, n + ks.start:n + ks.stop].unsqueeze(2).to_broadcast([P, len(ks), 2]), ALU.add, ALU.mult))

                def h_lo_tile(k):
                    vec.wait_ge(h_hi_ready, layer * KT + k + 1)
                    tt(h_lo[:, k], h_tmp[:, k % 2], h_hi[:, k].bitcast(F32), ALU.subtract).then_inc(h_ready, 1)
                    vec.wait_ge(h_ready, layer * KT + k + 1)

                for k in ks:
                    tt(h_tmp[:, k % 2], xT[:, k], x_rms, ALU.mult).then_inc(x_scaled, 1)
                    vec.wait_ge(x_scaled, layer * KT + k + 1)
                    if k > ks.start:
                        h_lo_tile(k - 1)
                h_lo_tile(ks.stop - 1)

            for g in range(ADA_START // 4):
                blk = group_block(g)
                vec.wait_ge(ada_turned, 4 * (g + 1))
                tt(mod[:, 0, blk:blk + 4, :], bank(A1, 8).rearrange("p (b v) -> p b v", b=4),
                   vecs[:, 1, blk:blk + 4].unsqueeze(2).to_broadcast([P, 4, 2]), ALU.add).then_inc(mod_ready, 4)
                vec.wait_ge(mod_ready, 4 * (g + 1))
                if g == 0:
                    for l in range(DEPTH):
                        own.done(V.tensor_scalar(halfw[:, l, 0:1], vecs[:, 0, 82 + l:83 + l], 0.5 * (1.0 - lam_init[l]), None, ALU.mult))
                        own.done(V.tensor_scalar(halfw[:, l, 1:2], vecs[:, 0, 80 + l:81 + l], 0.5, None, ALU.mult))
                    vec.wait_ge(lam_exp, 1)
                    for l in range(DEPTH):
                        own.done(tt(lam[:, l:l + 1], small[:, 41 + 2 * l:42 + 2 * l], small[:, 40 + 2 * l:41 + 2 * l], ALU.subtract))
                        own.done(V.tensor_scalar(lam[:, l:l + 1], lam[:, l:l + 1], -lam_init[l], None, ALU.add))
                if g == 1:
                    rms(0, 0)
                if g == 2:
                    vec.wait_ge(rms_copied, 1)
                if g == 7:
                    split_lo(0, 0)
                q = modulated_after(g)
                if q >= 0:
                    modulate(0, range(4 * q, 4 * q + 4))

            for layer in range(DEPTH):
                base = layer * LAYER_UNITS
                c0 = first_q(layer)
                own.finish()
                if layer:
                    split_lo(0, base)
                    rms(layer, 0)
                    vec.wait_ge(rms_copied, layer + 1)
                    modulate(layer, range(HALF))
                    split_lo(0, base + 1)
                    modulate(layer, range(HALF, KT))
                else:
                    split_lo(0, base + 1)
                vec.wait_ge(x_stored, 16 * (1 + layer * KT))
                own.done(V.memset(cin, 0.0))

                def table_step(s):
                    gx = decay[:, 0, 0, 0:NT * 16].rearrange("p (c n) -> p c n", c=NT)
                    e = decay[:, 0, 1, 0:NT * 16].rearrange("p (c n) -> p c n", c=NT)
                    tb = decay[:, 0, 2, 0:NT * 16].rearrange("p (c n) -> p c n", c=NT)
                    raw = bank(A0, P).rearrange("p (c n) -> p c n", c=NT)
                    if s == 0:
                        vec.wait_ge(ab_turned, layer + 1)
                        tt(gx, raw[:, :, 0:16], alog[:, 1, layer].unsqueeze(1).to_broadcast([P, NT, 16]),
                           ALU.add).then_inc(tab_g, 1)
                        vec.wait_ge(tab_g, layer + 1)
                    if s == 1:
                        vec.wait_ge(tab_soft, layer + 1)
                        own.done(V.scalar_tensor_tensor(gx, gx, 0.0, e, ALU.max, ALU.add))
                        own.done(tt(gx, gx, small[:, 48:64].unsqueeze(1).to_broadcast([P, NT, 16]), ALU.mult))
                        own.done(V.tensor_scalar(tab[:, TAB_BETA].rearrange("p x c h -> p c x h"),
                                                 tb.rearrange("p c (x h) -> p c x h", x=2), 0.5, 0.5, ALU.mult, ALU.add))
                        V.tensor_scalar(gx, gx, -1.0, None, ALU.mult).then_inc(tab_beta, 1)
                        vec.wait_ge(tab_beta, layer + 1)
                    if s == 2:
                        vec.wait_ge(tab_sums, layer + 1)
                        tabf = tab[:].rearrange("p k x c h -> p k (x c h)")
                        own.done(V.tensor_copy(tabf[:, TAB_G], bank(A1, 64)))
                        own.done(V.tensor_copy(decay[:, 0, 1, 0:64].rearrange("p (c x h) -> p c x h", c=NT, x=2),
                                               tab[:, TAB_G].rearrange("p x c h -> p c x h")))
                        tt(decay[:, 0, 3, 0:64], ps[:, A1, 64:128], tabf[:, TAB_G], ALU.subtract).then_inc(tab_last, 1)
                        vec.wait_ge(tab_last, layer + 1)

                def body(i, project, fill):
                    own.finish()

                    def h(off=-1, per=1, idx=1):
                        return nth(layer, i, off, per, idx)

                    def tap(x_, j):
                        t = (BQ, BK, BV)[x_]
                        s0 = tokens(layer, t) // N_CTX
                        acc = qkv[:, x_].rearrange("p (s n) -> p s n", s=2)[:, s0:]
                        if j == 0 and x_ == 0:
                            own.done(V.tensor_copy(convh[:], vecs[:, 2 + layer, 0:CONV_K * 24].rearrange(
                                "p (j x h) -> p j x h", j=CONV_K, x=3)[:, :, :, bass.ds(i, 1)].rearrange("p j x o -> p j (x o)")))
                            need(vec, v_turned, h())
                        src = cin[:, s0:, j:j + N_CTX]
                        w = convh[:, j, x_:x_ + 1]
                        if j == 0:
                            vec.wait_ge(evacuated, i * TILES + (layer * LAYER_TILES + 1 + t + 1))
                            own.done(V.tensor_scalar(acc, src, w, None, ALU.mult))
                        else:
                            m = V.scalar_tensor_tensor(acc, src, w, acc, ALU.mult, ALU.add)
                            if j == CONV_K - 1:
                                m.then_inc(conv_done, 1)
                                vec.wait_ge(conv_done, nth(layer, i, 0, 3, x_ + 1))
                            else:
                                own.done(m)

                    def silu(x_):
                        q0 = tokens(layer, x_)
                        vec.wait_ge(tanh_done, nth(layer, i, 0, 3, x_ + 1))
                        V.scalar_tensor_tensor(qkv[:, x_, q0:], th[:, q0:], 1.0, qkv[:, x_, q0:], ALU.add,
                                               ALU.mult).then_inc(qkv_ready, 1)
                        vec.wait_ge(qkv_ready, nth(layer, i, 0, 3, x_ + 1))

                    def rope(n):
                        dst = (a_k, a_q)[n]
                        vec.wait_ge(rot_done, nth(layer, i, 0, 2, n + 1))
                        need(vec, scored, nth_q(layer, i, 0, 0))
                        lat = dst[:, N_CTX:T]
                        own.done(tt(lat, bank(A0, N_CTX), sin_t, ALU.mult))
                        own.done(tt(a_raw, a_raw, cos_t, ALU.mult))
                        tt(lat, lat, a_raw, ALU.add).then_inc(rope_done, 1)
                        vec.wait_ge(rope_done, nth(layer, i, 0, 2, n + 1))

                    def z_silu(off, n):
                        z = (z_a, z_b)[n]
                        q0 = c0 * P
                        vec.wait_ge(evacuated, i * TILES + (layer * LAYER_TILES + 1 + off * TILES + ZA + n + 1))
                        V.scalar_tensor_tensor(z[:, q0:], th_z[:, q0:], 1.0, z[:, q0:], ALU.add, ALU.mult).then_inc(z_ready, 1)
                        vec.wait_ge(z_ready, nth(layer, i, off, 2, n + 1))

                    def decay_args():
                        own.done(V.tensor_copy(hcol[:].rearrange("p k x c -> p (k x c)"),
                                               tab[:].rearrange("p k x c h -> p (k x c) h")[:, :, bass.ds(i - 1, 1)]
                                               .rearrange("p n o -> p (n o)")))
                        vec.wait_ge(g_loaded, h() * 16)
                        need(vec, ob_turned, h(-2))
                        own.done(tt(decay, g_row, hcol[:, TAB_G].unsqueeze(3).to_broadcast([P, 2, NT, P]), ALU.subtract))
                        tt(decay, decay, far.unsqueeze(2).to_broadcast([P, 2, NT, P]), ALU.add).then_inc(decay_arg, 1)
                        vec.wait_ge(decay_arg, h())

                    def qk_sums():
                        vec.wait_ge(qk_squared, h())
                        V.tensor_reduce(small[:, c0:8], sq_b[:, c0:], AX, ALU.add).then_inc(qk_summed, 1)
                        vec.wait_ge(qk_summed, h())

                    def qk_norm():
                        vec.wait_ge(qk_rms, h())
                        flat = ps[:, G0:G0 + 2, :].rearrange("p b (c d) -> p (b c) d", d=P)
                        tt(qk_tok[:, c0:], flat[:, c0:], small[:, 8 + c0:16].unsqueeze(2).to_broadcast([P, 8 - c0, P]),
                           ALU.mult).then_inc(qk_normed, 1)
                        vec.wait_ge(qk_normed, h())

                    def gram_terms():
                        vec.wait_ge(grams, h())
                        vec.wait_ge(decay_ready, h())
                        for d in range(2):
                            own.go(V.scalar_tensor_tensor(att_T[:, d, c0:], quads(G3)[:, c0:], float(P) ** -0.5, decay[:, d, c0:],
                                                          ALU.mult, ALU.mult))
                            for cc in range(NT):
                                own.go(V.scalar_tensor_tensor(m_T[:, d, cc], quads(G2)[:, cc], hcol[:, TAB_BETA, d, cc:cc + 1],
                                                              decay[:, d, cc], ALU.mult, ALU.mult))
                        own.settle()
                        vec.sem_inc(m_ready, 1)

                    def substitute_backward(n):
                        if n == 0:
                            vec.wait_ge(blocks_in, h(-1, 16, 16))
                            vec.wait_ge(blk_identity, h())
                        substitute(V, own, 1, range(3 * n, 3 * n + 3))
                        if n == 4:
                            vec.sem_inc(blocks_solved, 1)

                    def turn_inv(d):
                        vec.wait_ge(inv_started, h(-1, 16, 16))
                        V.transpose(inv[:, d].rearrange("p c d -> p (c d)"),
                                    inv_T[:, d].rearrange("p c d -> p (c d)")).then_inc(inv_turned, 1)
                        vec.wait_ge(inv_turned, h(-1, 2, d + 1))

                    def q_decay():
                        vec.wait_ge(qk_T_ready, h())
                        for d in range(2):
                            m = V.scalar_tensor_tensor(q_dec[:, d, c0:], qk_T[:, c0:NT], float(P) ** -0.5, q_dec[:, d, c0:],
                                                       ALU.mult, ALU.mult)
                            if d == 0:
                                own.go(m)
                        m.then_inc(q_decayed, 1)
                        own.settle()
                        vec.wait_ge(q_decayed, h())

                    def mask_x(d, n):
                        vec.wait_ge(x_product[d], h(-1, LVL, n + 1))
                        tt(prod[:, d], quads(GX[d]), msk[:, n, d].unsqueeze(1).to_broadcast([P, NT, P]),
                           ALU.mult).then_inc(x_masked[d], 1)
                        vec.wait_ge(x_masked[d], h(-1, LVL, n + 1))

                    def merge(d, n):
                        vec.wait_ge(t_product[d], h(-1, LVL, n + 1))
                        if n < LVL - 1:
                            own.go(tt(inv[:, d], inv[:, d], quads(GX[d]), ALU.subtract))
                        tt(inv_T[:, d], inv_T[:, d], quads(GT[d]), ALU.subtract).then_inc(t_merged[d], 1)
                        vec.wait_ge(t_merged[d], h(-1, LVL, n + 1))
                        own.settle()

                    def state(j):
                        vec.wait_ge(s_product, h(-1, 3, j + 1))
                        for d in range(2):
                            ch = ORDER[d][j]
                            dst = states[:, d, j + 1]
                            if j == 0:
                                m = V.tensor_copy(dst, ps[:, GT[d], 0:P])
                            else:
                                m = V.scalar_tensor_tensor(dst, states[:, d, j], hcol[:, TAB_LAST, d, ch:ch + 1],
                                                           ps[:, GT[d], 0:P], ALU.mult, ALU.add)
                            if d == 0:
                                own.go(m)
                        m.then_inc(s_ready, 1)
                        own.settle()
                        vec.wait_ge(s_ready, h(-1, 3, j + 1))

                    def ob_sums():
                        vec.wait_ge(ob_squared, h())
                        V.tensor_reduce(small[:, 16 + c0:20], sq_b[:, c0:NT], AX, ALU.add).then_inc(ob_summed, 1)
                        vec.wait_ge(ob_summed, h())

                    def ob_norm():
                        vec.wait_ge(ob_rms, h())
                        tt(o_b[:, c0:], quads(G0)[:, c0:], small[:, 20 + c0:24].unsqueeze(2).to_broadcast([P, NT - c0, P]),
                           ALU.mult).then_inc(ob_normed, 1)
                        vec.wait_ge(ob_normed, h())

                    def y_out(which):
                        turned, src, z, yy, ready, stored = (
                            (oa_turned, A0, z_a, y_a, ya_ready, ya_stored), (ob_turned, G1, z_b, y_b, yb_ready, yb_stored))[which]
                        vec.wait_ge(turned, h())
                        need(vec, stored, h(-2) * 16)
                        V.scalar_tensor_tensor(yy[:, c0 * P:], ps[:, src, c0 * P:], halfw[:, layer, which:which + 1],
                                               z[:, c0 * P:], ALU.mult, ALU.mult).then_inc(ready, 1)
                        vec.wait_ge(ready, h())

                    def a_max(n):
                        qt = q_tiles[layer][n]
                        keys = T if qt >= 2 else N_CTX
                        vec.wait_ge(scored, nth_q(layer, i, -1, n + 1))
                        own.done(V.tensor_reduce(small[:, 32:34], ps[:, A0:A0 + 2, 0:keys], AX, ALU.max))
                        V.tensor_scalar(small[:, 34:36], small[:, 32:34], -0.125, None, ALU.mult).then_inc(maxed, 1)
                        vec.wait_ge(maxed, nth_q(layer, i, -1, n + 1))

                    def a_mix(n):
                        qt = q_tiles[layer][n]
                        keys = T if qt >= 2 else N_CTX
                        vec.wait_ge(exped, nth_q(layer, i, -1, n + 1))
                        own.done(V.reciprocal(small[:, 38:40], small[:, 36:38]))
                        own.done(V.tensor_scalar(prob[:, 1, 0:keys], prob[:, 1, 0:keys], small[:, 39:40], lam[:, layer:layer + 1],
                                                 ALU.mult, ALU.mult))
                        V.scalar_tensor_tensor(prob[:, 0, 0:keys], prob[:, 0, 0:keys], small[:, 38:39], prob[:, 1, 0:keys],
                                               ALU.mult, ALU.add).then_inc(mixed, 1)
                        vec.wait_ge(mixed, nth_q(layer, i, -1, n + 1))

                    def oa_sums():
                        vec.wait_ge(oa_squared, h())
                        V.tensor_reduce(small[:, 24 + c0:28], sq_a[:, 0, c0 * P:].rearrange("p (c d) -> p c d", d=P), AX,
                                        ALU.add).then_inc(oa_summed, 1)
                        vec.wait_ge(oa_summed, h())

                    def oa_norm():
                        vec.wait_ge(oa_rms, h())
                        tt(o_a[:, c0:], o_a[:, c0:], small[:, 28 + c0:32].unsqueeze(2).to_broadcast([P, NT - c0, P]),
                           ALU.mult).then_inc(oa_normed, 1)
                        vec.wait_ge(oa_normed, h())

                    def ada(k):
                        lay, firstb = ada_block(layer, k)
                        mod_column(i * ADA_IN[layer] + (ada_before(layer) + k + 1), lay, i * 2 + (firstb + k % 2))

                    def y_lo(g):
                        vec.wait_ge(y_hi_ready, layer * Y_STEPS + g + 1)
                        lo = h_lo[:, Y_GROUPS[g], c0 * P:]
                        tt(lo, lo.bitcast(F32), h_hi[:, Y_GROUPS[g], c0 * P:].bitcast(F32), ALU.subtract).then_inc(y_split, 1)

                    def y_lo_last(which):
                        k = OUT_HEADS + HEADS * which
                        vec.wait_ge(y_hi_ready, layer * Y_STEPS + len(Y_GROUPS) + which + 1)
                        tt(h_lo[:, k, c0 * P:], (y_a, y_b)[which][:, c0 * P:], h_hi[:, k, c0 * P:].bitcast(F32),
                           ALU.subtract).then_inc(y_split, 1)

                    def part_add(n):
                        vec.wait_ge(part_loaded[n % 2], 16 * (layer * KT // 2 + n // 2 + 1))
                        vec.wait_ge(w_used, first + 2 * n + 2)
                        add_product(n, x_part[n % 2])
                        vec.wait_ge(out_added, layer * 2 * KT + n + 1)

                    plan = {}

                    def put(s, f, *a):
                        plan.setdefault(s, []).append((f, a))

                    nq = len(q_tiles[layer])
                    if not project:
                        for g in range(len(Y_GROUPS)):
                            put((3, 4, 6, 7)[g], y_lo, g)
                        put(40, y_lo_last, 0)
                    if fill:
                        put(0, decay_args)
                        put(1, z_silu, -1, 1)
                        put(2, qk_sums)
                        for n in range(nq):
                            put(3 + 8 * n, a_max, n)
                            put(6 + 8 * n, a_mix, n)
                        put(5, qk_norm)
                        put(9, gram_terms)
                        put(11, q_decay)
                        for n in range(5):
                            put(15 + n, substitute_backward, n)
                        put(24, turn_inv, 0)
                        put(25, turn_inv, 1)
                        for n in range(LVL):
                            put(27 + 4 * n, mask_x, 0, n)
                            put(28 + 4 * n, mask_x, 1, n)
                            put(29 + 4 * n, merge, 0, n)
                            put(30 + 4 * n, merge, 1, n)
                        for j in range(3):
                            put(44 + 4 * j, state, j)
                        put(57, ob_sums)
                        put(60, ob_norm)
                        put(62, y_out, 1)
                        put(3 + 8 * nq, oa_sums)
                        put(5 + 8 * nq, oa_norm)
                        put(39, y_out, 0)
                    if project:
                        for x_ in range(3):
                            for j in range(CONV_K):
                                put(8 * x_ + 9 + j, tap, x_, j)
                            put(8 * x_ + 15, silu, x_)
                        put(41, rope, 0)
                        put(61, rope, 1)
                        put(58, z_silu, 0, 0)
                        for k in range(ADA_IN[layer]):
                            put(45 + 3 * k, ada, k)
                        if isinstance(i, int) and i == 0:
                            put(2, table_step, 0)
                            put(4, table_step, 1)
                            put(6, table_step, 2)
                    if not project:
                        put(62, y_lo_last, 1)
                        for n in range(KT):
                            put(out_slot(n), part_add, n)
                        for u in range(OUT_UNITS):
                            put(piece_slot(2 * u), split_lo, 0, first + u + 1, OUT_HEADS if u < OUT_UNITS - 1 else HALF)
                    for s in range(SLOTS):
                        if project and s % 4 == 2:
                            split_lo(i, base + 2 + s // 4 + 1)
                        for f, a in plan.get(s, ()):
                            f(*a)
                    own.finish()

                first = base + 2 + HEADS * UNITS

                def add_product(n, dst):
                    for v in range(c0 // 2, 2):
                        seg = slice(v * N_CTX, (v + 1) * N_CTX)
                        m = V.scalar_tensor_tensor(dst[:, seg], ps[:, PJ + n % 2, seg], mod[:, layer, 2 * KT + n, v:v + 1],
                                                   dst[:, seg], ALU.mult, ALU.add)
                        if v == 0:
                            own.go(m)
                    m.then_inc(out_added, 1)
                    if c0 == 0:
                        own.settle()

                split_lo(0, base + 2)
                own.finish()
                heads(vec, layer, body)

                own.finish()
                own.done(V.memset(sq_sum, 0.0))

                def add_square(n):
                    vec.wait_ge(x_squared, layer * KT + n + 1)
                    tt(sq_sum[:, c0 * P:], sq_sum[:, c0 * P:], sq_tiles[n % 2][:, c0 * P:], ALU.add).then_inc(sums_ready, 1)
                    vec.wait_ge(sums_ready, layer * KT + n + 1)

                for n in range(KT):
                    if n % 4 == 0:
                        if n // 4 + 1 < LAST_UNITS:
                            split_lo(0, first + OUT_UNITS + n // 4 + 1)
                        vec.wait_ge(old_loaded[n // 4], 16 * (layer + 1))
                    vec.wait_ge(last_product, layer * KT + n + 1)
                    add_product(n, xT[:, n])
                    vec.wait_ge(out_added, (2 * layer + 1) * KT + n + 1)
                    if n >= 1:
                        add_square(n - 1)
                add_square(KT - 1)

            rms(DEPTH, N_CTX // P)
            vec.wait_ge(rms_copied, DEPTH + 1)
            for k in range(KT):
                V.scalar_tensor_tensor(xT[:, k, N_CTX:], xT[:, k, N_CTX:], vecs[:, 0, 64 + k:65 + k], x_rms[:, N_CTX:],
                                       ALU.mult, ALU.mult).then_inc(fin_scaled, 1)

        @block.gpsimd
        def _(pool):
            own = Count(pool, pool_step)
            G = nc.gpsimd
            pool.dma_start(msk[:].rearrange("p n x d -> p (n x d)"), masks).then_inc(masks_loaded, 16)
            G.memset(zeros, 0.0).then_inc(zeros_set, 1)
            pool.wait_ge(zeros_set, 1)
            pool.dma_start(chunk_rows(s_dram), zeros.rearrange("p (x n) -> p x n", n=P)).then_inc(zeros_out, 16)
            pool.wait_ge(zeros_out, 16)
            pool.wait_ge(staged, 1)

            def power(dst, src, n, scale, eps, signal, value):
                own.note()
                own.done(G.tensor_scalar(dst, src, scale, eps, ALU.mult, ALU.add))
                G.tensor_tensor(dst, dst, minus_half[:, 0:n], ALU.pow).then_inc(signal, 1)
                pool.wait_ge(signal, value)

            def rms(n, c0):
                pool.wait_ge(sums_copied, n) if n else pool.wait_ge(x_measured, NT)
                power(small[:, 44 + c0:48], small[:, 44 + c0:48], NT - c0, 1.0 / D, NORM_EPS, rms_ready, n + 1)

            for layer in range(DEPTH):
                c0 = first_q(layer)
                own.finish()
                rms(layer, 0)

                def body(i, project, fill):
                    own.finish()
                    if not fill:
                        return

                    def h(off=-1, per=1, idx=1):
                        return nth(layer, i, off, per, idx)

                    pool.wait_ge(qk_summed, h())
                    power(small[:, 8 + c0:16], small[:, c0:8], 8 - c0, 1.0, 4e-6, qk_rms, h())
                    pool.wait_ge(qk_normed, h())
                    need(pool, w_product, h(-2, 2, 2))
                    need(pool, s_product, h(-2, 3, 3))
                    for d in range(2):
                        for n, dst in ((TAB_GROW, k_grow), (TAB_END, k_end)):
                            m = G.tensor_tensor(dst[:, d], qk_tok[:, NT:], hcol[:, n, d].unsqueeze(2).to_broadcast([P, NT, P]),
                                                ALU.mult)
                            if (d, n) != (1, TAB_END):
                                own.go(m)
                    m.then_inc(k_scaled, 1)
                    own.settle()
                    pool.wait_ge(k_scaled, h())
                    own.done(G.memset(blk_s, 0.0))
                    G.memset(blk_s[:, 0::BLK + 1], 1.0).then_inc(blk_identity, 1)
                    pool.wait_ge(blk_identity, h())
                    pool.wait_ge(blocks_in, h(-1, 16, 16))
                    substitute(G, own, 0, range(BLK - 1))
                    pool.sem_inc(blocks_solved, 1)
                    pool.wait_ge(oa_summed, h())
                    power(small[:, 28 + c0:32], small[:, 24 + c0:28], NT - c0, 1.0 / P, SUBLN_EPS, oa_rms, h())
                    pool.wait_ge(ob_summed, h())
                    power(small[:, 20 + c0:24], small[:, 16 + c0:20], NT - c0, 1.0 / P, NORM_EPS, ob_rms, h())
                    own.finish()

                own.finish()
                heads(pool, layer, body)

            own.finish()
            rms(DEPTH, N_CTX // P)

        @block.tensor
        def _(pe):
            mm = nc.tensor.matmul
            turn = nc.tensor.transpose

            pe.wait_ge(consts_loaded, 16)
            pe.wait_ge(rows_loaded, 16 * 12)
            for b in range(4):
                last = turn(ps[:, A0, b * P:(b + 1) * P], rows_in[:, b], ident)
            last.then_inc(setup_turned, 1)

            def turn_x(n):
                pe.wait_ge(x_loaded[n % 2], 16 * (n // 2 + 1))
                for q in range(4):
                    if n >= 1:
                        pe.wait_ge(x_evacuated, (n - 1) * 4 + q + 1)
                    for k in range(4 * q, 4 * q + 4):
                        last = turn(ps[:, G0 + q, (k % 4) * P:(k % 4 + 1) * P], x_in[:, n % 2, k * P:(k + 1) * P], ident)
                    last.then_inc(x_turned, 1)

            def ada_multiply(slots, loads, prior):
                need(pe, ada_copied, prior)
                for half in range(2):
                    pe.wait_ge(slots[half][1], loads[half])
                    for k in range(HALF):
                        kt = half * HALF + k
                        j = kt % 4
                        last = mm(ps[32 * j:32 * j + 32, A0, 0:P], c_T[:, kt, :], slots[half][0][:, k, :],
                                  start=kt < 4, stop=kt >= KT - 4)
                        if k == HALF - 1:
                            last.then_inc(ada_used, 1)

            def ada_turn(value):
                pe.wait_ge(ada_copied, value)
                need(pe, mod_ready, value - 1)
                mm(bank(A1, 2), ada_sb[:], sel, start=True, stop=True).then_inc(ada_turned, 1)

            pe.wait_ge(staged, 2)
            turn_x(0)
            turn_x(1)

            def spread_rms(n, c0, bank_):
                pe.wait_ge(diag_ready, n + 1)
                mm(ps[:, bank_, c0 * P:], ones, diag[:, c0 * P:], start=True, stop=True).then_inc(rms_spread, 1)

            def rms(n, c0):
                pe.wait_ge(sums_ready, n * KT)
                for cc in range(c0, NT):
                    last = mm(ps[:, A0, cc:cc + 1], sq_sum[:, cc * P:(cc + 1) * P], ones[:, 0:1], start=True, stop=True)
                last.then_inc(sums_turned, 1)
                spread_rms(n, c0, A1)

            for g in range(ADA_START // 4):
                for pair in range(8):
                    u = 8 * g + pair
                    pe.wait_ge(ada_loaded[u % RING], 16 * (u // RING + 1))
                    wide = ada_ring[u % RING].rearrange("p k n -> p (k n)").rearrange("p (k n) -> p k n", k=2)
                    for k in range(2):
                        kt = 2 * pair + k
                        j = kt % 4
                        last = mm(ps[32 * j:32 * j + 32, A0, :], c_T[:, kt, :], wide[:, k, :],
                                  start=kt < 4, stop=kt >= KT - 4)
                    last.then_inc(ada_used, 1)
                if g == 2:
                    pe.wait_ge(x_evacuated, 4 * NT)
                    spread_rms(0, 0, G1)
                pe.wait_ge(ada_copied, 4 * (g + 1))
                need(pe, mod_ready, 4 * g)
                for b in range(4):
                    last = mm(ps[:, A1, 2 * b:2 * b + 2], ada_wide[:, g % 2, b * P:(b + 1) * P], sel, start=True, stop=True)
                last.then_inc(ada_turned, 4)
                if g < 2:
                    turn_x(2 + g)

            for layer in range(DEPTH):
                base = layer * LAYER_UNITS
                c0 = first_q(layer)
                if layer:
                    rms(layer, 0)

                def unit_piece(u, bank_, t0, half, ks, signal=None):
                    s = u % 2
                    for k in ks:
                        kt = half * HALF + k
                        o = ps[:, bank_, t0:]
                        mm(o, w_hi[:, s, k], h_hi[:, kt, t0:], start=kt == 0, stop=False)
                        mm(o, w_hi[:, s, k], h_lo[:, kt, t0:], start=False, stop=False)
                        last = mm(o, w_lo[:, s, k], h_hi[:, kt, t0:], start=False, stop=kt == KT - 1)
                    return last

                if layer == 1:
                    pe.wait_ge(evacuated, LAYER_TILES)
                for half in range(2):
                    pe.wait_ge(w_split, base + half + 1)
                    for k in range(HALF):
                        pe.wait_ge(h_ready, layer * KT + half * HALF + k + 1)
                        last = unit_piece(base + half, PJ, 0, half, [k])
                    last.then_inc(w_used, 1)

                def table_step(s):
                    if s == 0:
                        pe.wait_ge(evacuated, layer * LAYER_TILES + 1)
                        for cc in range(NT):
                            last = turn(ps[:, A0, cc * 32:(cc + 1) * 32], th[96:128, cc * P:(cc + 1) * P], ident[96:128, 96:128])
                        last.then_inc(ab_turned, 1)
                    if s == 1:
                        pe.wait_ge(tab_beta, layer + 1)
                        gx = decay[:, 0, 0, 0:NT * 16].rearrange("p (c n) -> p c n", c=NT)
                        for n in range(4):
                            d = n % 2
                            lhs = cst[:, C_TRI + d * P:C_TRI + (d + 1) * P] if n < 2 else ones
                            last = mm(ps[:, A1, n * 32:(n + 1) * 32], lhs, gx[:, :, 8 * d:8 * d + 8], start=True, stop=True)
                        last.then_inc(tab_sums, 1)
                    if s == 2:
                        pe.wait_ge(tab_ready, layer + 1)
                        for cc in range(NT):
                            last = turn(ps[0:16, A0, cc * P:(cc + 1) * P], decay[:, 0, 1, 16 * cc:16 * cc + 16], ident)
                        last.then_inc(tab_rows, 1)

                def body(i, project, fill):
                    def h(off=-1, per=1, idx=1):
                        return nth(layer, i, off, per, idx)

                    def turn_qk():
                        pe.wait_ge(qkv_ready, h(-1, 3, 3))
                        need(pe, yb_ready, h(-2))
                        for n in range(c0, 8):
                            x_, cc = n // NT, n % NT
                            last = turn(ps[:, G0 + x_, cc * P:(cc + 1) * P], qkv[:, x_, cc * P:(cc + 1) * P], ident)
                        last.then_inc(qk_turned, 1)

                    def turn_v():
                        for cc in range(NT):
                            last = turn(ps[:, G2, cc * P:(cc + 1) * P], qkv[:, 2, cc * P:(cc + 1) * P], ident)
                        last.then_inc(v_turned, 1)

                    def turn_back():
                        pe.wait_ge(qk_normed, h())
                        for n in range(c0, 8):
                            last = turn(ps[:, G0 + n // NT, (n % NT) * P:(n % NT + 1) * P], qk_tok[:, n], ident)
                        last.then_inc(qk_returned, 1)

                    def gram():
                        pe.wait_ge(qk_T_ready, h())
                        pe.wait_ge(vb_ready, h())
                        for cc in range(NT):
                            last = mm(quads(G2)[:, cc], qk_T[:, NT + cc], qk_T[:, NT + cc], start=True, stop=True)
                        for cc in range(c0, NT):
                            last = mm(quads(G3)[:, cc], qk_T[:, NT + cc], qk_T[:, cc], start=True, stop=True)
                        last.then_inc(grams, 1)

                    def times_m(d, n):
                        if n == 0:
                            pe.wait_ge(inv_turned, h(-1, 2, d + 1))
                        else:
                            pe.wait_ge(t_merged[d], h(-1, LVL, n))
                        for cc in range(NT):
                            last = mm(quads(GX[d])[:, cc], m_T[:, d, cc], inv[:, d, cc], start=True, stop=True)
                        last.then_inc(x_product[d], 1)

                    def times_inv(d, n):
                        pe.wait_ge(x_masked[d], h(-1, LVL, n + 1))
                        for cc in range(NT):
                            if n < LVL - 1:
                                mm(quads(GX[d])[:, cc], inv_T[:, d, cc], prod[:, d, cc], start=True, stop=True)
                            last = mm(quads(GT[d])[:, cc], prod[:, d, cc], inv_T[:, d, cc], start=True, stop=True)
                        last.then_inc(t_product[d], 1)

                    def w_mul(d):
                        pe.wait_ge(t_merged[d], h(-1, LVL, LVL))
                        pe.wait_ge(k_scaled, h())
                        for cc in range(NT):
                            last = mm(quads(GX[d])[:, cc], k_grow[:, d, cc], inv_T[:, d, cc], start=True, stop=True)
                        last.then_inc(w_product, 1)

                    def v_mul(j):
                        if j == 0:
                            pe.wait_ge(w_ready, h(-1, 2, 2))
                        else:
                            pe.wait_ge(s_ready, h(-1, 3, j))
                        for d in range(2):
                            ch = ORDER[d][j]
                            last = mm(ps[:, GT[d], 0:P], inv_T[:, d, ch], v_tok[:, ch], start=True, stop=j == 0)
                            if j:
                                last = mm(ps[:, GT[d], 0:P], w_T[:, d, ch], states[:, d, j], start=False, stop=True)
                        last.then_inc(v_product, 1)

                    def s_mul(j):
                        pe.wait_ge(v_ready, h(-1, 4, j + 1))
                        for d in range(2):
                            ch = ORDER[d][j]
                            last = mm(ps[:, GT[d], 0:P], k_end[:, d, ch], v_new[:, d, ch], start=True, stop=True)
                        last.then_inc(s_product, 1)

                    def o_mul():
                        pe.wait_ge(v_ready, h(-1, 4, 4))
                        pe.wait_ge(q_decayed, h())
                        for cc in range(c0, NT):
                            terms = []
                            for d in range(2):
                                terms.append((att_T[:, d, cc], v_new[:, d, cc]))
                                j = ORDER[d].index(cc)
                                if j:
                                    terms.append((q_dec[:, d, cc], states[:, d, j]))
                            for n, (a, b) in enumerate(terms):
                                last = mm(quads(G0)[:, cc], a, b, start=n == 0, stop=n == len(terms) - 1)
                        last.then_inc(ob_product, 1)

                    def turn_ob():
                        pe.wait_ge(ob_normed, h())
                        for cc in range(c0, NT):
                            last = turn(quads(G1)[:, cc], o_b[:, cc], ident)
                        last.then_inc(ob_turned, 1)

                    def turn_va():
                        need(pe, rope_done, h(-1, 2, 2))
                        for cc in range(NT):
                            last = turn(quads(A0)[:, cc], a_v[:, cc * P:(cc + 1) * P], ident)
                        last.then_inc(va_turned, 1)

                    def score(n):
                        qt = q_tiles[layer][n]
                        keys = T if qt >= 2 else N_CTX
                        if n == 0:
                            pe.wait_ge(va_ready, h())
                            pe.wait_ge(mod_ready, ada_before(layer) + i * ADA_IN[layer])
                        else:
                            pe.wait_ge(oa_copied, nth_q(layer, i, -1, n))
                        for m in range(2):
                            r = slice(64 * m, 64 * m + 64)
                            last = mm(bank(A0 + m, keys), a_q[r, qt * P:(qt + 1) * P], a_k[r, 0:keys], start=True, stop=True)
                        last.then_inc(scored, 1)

                    def turn_p(n):
                        kt = NT if q_tiles[layer][n] >= 2 else 2
                        pe.wait_ge(mixed, nth_q(layer, i, -1, n + 1))
                        for cc in range(kt):
                            last = turn(quads(A0)[:, cc], prob[:, 0, cc * P:(cc + 1) * P], ident)
                        last.then_inc(p_turned, 1)

                    def attend(n):
                        kt = NT if q_tiles[layer][n] >= 2 else 2
                        pe.wait_ge(p_copied, nth_q(layer, i, -1, n + 1))
                        for cc in range(kt):
                            last = mm(bank(A1, P), prob_T[:, cc], va_tok[:, cc], start=cc == 0, stop=cc == kt - 1)
                        last.then_inc(oa_product, 1)

                    def turn_oa():
                        pe.wait_ge(oa_normed, h())
                        for cc in range(c0, NT):
                            last = turn(quads(A0)[:, cc], o_a[:, cc], ident)
                        last.then_inc(oa_turned, 1)

                    def rotate(n):
                        t = (AK, AQ)[n]
                        pe.wait_ge(evacuated, i * TILES + (layer * LAYER_TILES + 1 + t + 1))
                        if isinstance(i, int) and i == 0:
                            pe.wait_ge(rows_copied, layer + 1)
                        elif n == 0:
                            pe.wait_ge(ya_ready, h())
                        mm(bank(A0, N_CTX), rot, a_raw, start=True, stop=True).then_inc(rot_done, 1)

                    def ada(k):
                        if k == 0:
                            pe.wait_ge(rope_done, nth(layer, i, 0, 2, 1))
                        first_loads = ada_before(layer)
                        at_start = [len([u for u in range(2 * ADA_START) if u % 6 == 4 + hf]) for hf in range(2)]
                        n = first_loads - ADA_START + k
                        loads = [i * (16 * ADA_IN[layer]) + 16 * (at_start[hf] + n + 1) for hf in range(2)]
                        sl = [(ada_raw[:, hf], ada_loaded[4 + hf]) for hf in range(2)]
                        v = i * ADA_IN[layer] + (first_loads + k)
                        ada_multiply(sl, loads, v)

                    def ada_t(k):
                        ada_turn(i * ADA_IN[layer] + (ada_before(layer) + k + 1))

                    plan = {}

                    def put(s, f, *a):
                        plan.setdefault(s, []).append((f, a))

                    nq = len(q_tiles[layer])
                    if fill:
                        put(0, turn_qk)
                        put(1, turn_v)
                        put(0, turn_va)
                        put(5, turn_back)
                        put(8, gram)
                        for n in range(LVL):
                            put(27 + 4 * n, times_m, 0, n)
                            put(28 + 4 * n, times_m, 1, n)
                            put(29 + 4 * n, times_inv, 0, n)
                            put(30 + 4 * n, times_inv, 1, n)
                        put(39, w_mul, 0)
                        put(40, w_mul, 1)
                        for j in range(4):
                            put(42 + 4 * j, v_mul, j)
                            if j < 3:
                                put(44 + 4 * j, s_mul, j)
                        put(56, o_mul)
                        put(61, turn_ob)
                        for n in range(nq):
                            put(2 + 8 * n, score, n)
                            put(7 + 8 * n, turn_p, n)
                            put(9 + 8 * n, attend, n)
                        put(6 + 8 * nq, turn_oa)
                    if project:
                        put(40, rotate, 0)
                        put(60, rotate, 1)
                        for k in range(ADA_IN[layer]):
                            put(42 + 3 * k, ada, k)
                            put(44 + 3 * k, ada_t, k)
                        if isinstance(i, int) and i == 0:
                            put(2, table_step, 0)
                            put(5, table_step, 1)
                            put(8, table_step, 2)
                    def out_piece(p):
                        u, half, n = first + p // 2, p // 2 % 2, p // 4
                        if p % 2 == 0:
                            pe.wait_ge(w_split, u + 1)
                        if p == 0:
                            pe.wait_ge(evacuated, (layer + 1) * LAYER_TILES)
                        if p % 4 == 0 and n >= 2:
                            pe.wait_ge(out_added, layer * 2 * KT + n - 1)
                        for k in (range(0, 4), range(4, OUT_HEADS))[p % 2]:
                            kt = half * HALF + k
                            if n == 0:
                                pe.wait_ge(y_split, layer * Y_STEPS + y_group_of[kt] + 1)
                            o = ps[:, PJ + n % 2, c0 * P:]
                            mm(o, w_hi[:, u % 2, k], h_hi[:, kt, c0 * P:], start=kt == 0, stop=False)
                            mm(o, w_hi[:, u % 2, k], h_lo[:, kt, c0 * P:], start=False, stop=False)
                            last = mm(o, w_lo[:, u % 2, k], h_hi[:, kt, c0 * P:], start=False, stop=kt == HALF + OUT_HEADS - 1)
                        if p % 2:
                            last.then_inc(w_used, 1)

                    for s in range(SLOTS):
                        if not project:
                            for p in range(2 * OUT_UNITS):
                                if piece_slot(p) == s:
                                    out_piece(p)
                        if project:
                            k = s // 4
                            t, half = k // 2, k % 2
                            if s % 4 == 0:
                                pe.wait_ge(w_split, i * UNITS + (base + 2 + k + 1))
                                if half == 0:
                                    pe.wait_ge(evacuated, i * TILES + (layer * LAYER_TILES + 1 + t - 1))
                            last = unit_piece(base + 2 + k, PJ + (1 + t) % 2, tokens(layer, t), half,
                                              [2 * (s % 4), 2 * (s % 4) + 1])
                            if s % 4 == 3:
                                last.then_inc(w_used, 1)
                        for f, a in plan.get(s, ()):
                            f(*a)

                first = base + 2 + HEADS * UNITS
                heads(pe, layer, body)

                pe.wait_ge(y_split, Y_STEPS * (layer + 1))
                for n in range(KT):
                    u, col = first + OUT_UNITS + n // 4, n % 4
                    if col == 0:
                        pe.wait_ge(w_split, u + 1)
                    pe.wait_ge(out_added, (2 * layer + 1) * KT + n - 1)
                    for m, k in enumerate((OUT_HEADS, OUT_HEADS + HEADS)):
                        hi, lo = [w[:, u % 2].rearrange("p k n -> p (k n)")[:, (4 * m + col) * P:(4 * m + col + 1) * P]
                                  for w in (w_hi, w_lo)]
                        o = ps[:, PJ + n % 2, c0 * P:]
                        mm(o, hi, h_hi[:, k, c0 * P:], start=m == 0, stop=False)
                        mm(o, hi, h_lo[:, k, c0 * P:], start=False, stop=False)
                        last = mm(o, lo, h_hi[:, k, c0 * P:], start=False, stop=m == 1)
                    last.then_inc(last_product, 1)
                    if col == 3:
                        pe.wait_ge(last_product, layer * KT + n + 1)
                        pe.sem_inc(w_used, 1)

            rms(DEPTH, N_CTX // P)
            for n in range(2):
                for q in range(4):
                    if n == 1:
                        pe.wait_ge(fin_copied, q + 1)
                    for k in range(4 * q, 4 * q + 4):
                        pe.wait_ge(fin_scaled, k + 1)
                        last = turn(ps[:, G0 + q, (k % 4) * P:(k % 4 + 1) * P],
                                    xT[:, k, (2 + n) * P:(3 + n) * P], ident)
                    last.then_inc(fin_turned, 1)


_INS = ['x', 'c', 'ctx', 'c_ctx', 'w_ada', 'b_ada', 'norm_w', 'w_in', 'conv_w', 'dn_a_log', 'dn_dt_bias',
        'dn_norm_w', 'diff_lambda', 'subln_w', 'w_out', 'final_norm_w']


def kernel(**inputs):
    import ml_dtypes
    import concourse.bacc as _bacc
    from concourse.bass_utils import run_bass_kernel_spmd as _run

    consts, masks = shape_constants()
    nc = _bacc.Bacc("TRN2", target_bir_lowering=False, num_devices=1)
    arrays, args = {}, []
    for name in _INS:
        arrays[f"in_{name}"] = np.ascontiguousarray(inputs[name])
    arrays["in_consts"] = consts
    arrays["in_masks"] = masks.astype(ml_dtypes.bfloat16)
    for name, a in arrays.items():
        args.append(nc.dram_tensor(name, a.shape, mybir.dt.from_np(a.dtype), kind="ExternalInput").ap())
    args.append(nc.dram_tensor("out", inputs["x"].shape, F32, kind="ExternalOutput").ap())
    build_trunk(nc, *args)
    r = _run(nc, [arrays], core_ids=[0])
    return r.results[0]["out"]
```
